# Optimizing a Trainium2 kernel written in Bass

```python
import jax, jax.numpy as jnp
from jax import lax
import numpy as np

D_MODEL = 1024
BATCH = 1
SEQ = 1024
DEPTH = 1

PLE_DIM = 256
D_CONF = D_MODEL // 2
D_SC = D_MODEL // 2
N_GROUPS_CONF = 8
N_GROUPS_SC = 8
CONF_KERNEL = 31
SC_KERNEL = 3
FFN_KERNEL = 3
D_FF = 2816
EPS = 1e-6

W_IN_COLS = 2 * D_CONF + 3 * D_SC + 2 * D_MODEL


def rmsnorm(x, g):
    xf = x.astype(jnp.float32)
    y = xf * lax.rsqrt(jnp.mean(xf * xf, axis=-1, keepdims=True) + EPS)
    return (y * g.astype(jnp.float32)).astype(x.dtype)

def layernorm(x, g, b):
    xf = x.astype(jnp.float32)
    mu = jnp.mean(xf, axis=-1, keepdims=True)
    var = jnp.mean(jnp.square(xf - mu), axis=-1, keepdims=True)
    y = (xf - mu) * lax.rsqrt(var + EPS)
    return (y * g.astype(jnp.float32) + b.astype(jnp.float32)).astype(x.dtype)

def causal_dwconv(u, w):
    k, c = w.shape
    return lax.conv_general_dilated(
        u, w[:, None, :].astype(u.dtype),
        window_strides=(1,), padding=[(k - 1, 0)],
        dimension_numbers=("NWC", "WIO", "NWC"),
        feature_group_count=c)

def first_inputs(seed: int = 0) -> dict:
    key = jax.random.key(seed)
    ks = jax.random.split(key, 24)
    f32 = jnp.float32

    def dense(k, shape, fan_in):
        return jax.random.normal(k, shape, f32) * (fan_in ** -0.5)

    def gain(k, shape):
        return 1.0 + 0.05 * jax.random.normal(k, shape, f32)

    def small(k, shape):
        return 0.02 * jax.random.normal(k, shape, f32)

    L = DEPTH
    return {
        "x": jax.random.normal(ks[0], (BATCH, SEQ, D_MODEL), f32),
        "p": jax.random.normal(ks[1], (DEPTH, BATCH, SEQ, PLE_DIM), f32),
        "g_mix": gain(ks[2], (L, D_MODEL)),
        "w_in": dense(ks[3], (L, D_MODEL, W_IN_COLS), D_MODEL),
        "b_gate": small(ks[4], (L, 2 * D_MODEL)),
        "conv_a_w": dense(ks[5], (L, CONF_KERNEL, D_CONF), CONF_KERNEL),
        "conv_a_b": small(ks[6], (L, D_CONF)),
        "ln_a_g": gain(ks[7], (L, D_CONF)),
        "ln_a_b": small(ks[8], (L, D_CONF)),
        "w_a_out": dense(ks[9], (L, D_CONF, D_MODEL), D_CONF),
        "conv_b_w": dense(ks[10], (L, SC_KERNEL, D_SC), SC_KERNEL),
        "w_b_out": dense(ks[11], (L, D_SC, D_MODEL), D_SC),
        "w_o": dense(ks[12], (L, D_MODEL, D_MODEL), D_MODEL),
        "g_ffn": gain(ks[13], (L, D_MODEL)),
        "w_up": dense(ks[14], (L, D_MODEL, 2 * D_FF), D_MODEL),
        "conv_f_w": dense(ks[15], (L, FFN_KERNEL, D_FF), FFN_KERNEL),
        "conv_f_b": small(ks[16], (L, D_FF)),
        "w_down": dense(ks[17], (L, D_FF, D_MODEL), D_FF),
        "g_ple": gain(ks[18], (L, D_MODEL)),
        "w_ple": dense(ks[19], (L, PLE_DIM, D_MODEL), PLE_DIM),
        "w_ple_gate": dense(ks[20], (L, D_MODEL, D_MODEL), D_MODEL),
        "g_final": gain(ks[21], (D_MODEL,)),
    }

def first_block(x, p, g_mix, w_in, b_gate, conv_a_w, conv_a_b, ln_a_g, ln_a_b, w_a_out,
              conv_b_w, w_b_out, w_o, g_ffn, w_up, conv_f_w, conv_f_b, w_down,
              g_ple, w_ple, w_ple_gate, g_final):
    o1 = D_CONF
    o2 = o1 + D_CONF
    o3 = o2 + D_SC
    o4 = o3 + D_SC
    o5 = o4 + D_SC
    o6 = o5 + D_MODEL
    for i in range(DEPTH):
        h = rmsnorm(x, g_mix[i])
        z = jnp.einsum("bsd,dn->bsn", h, w_in[i])
        a_val, a_gt = z[..., :o1], z[..., o1:o2]
        sc_b, sc_c, sc_v = z[..., o2:o3], z[..., o3:o4], z[..., o4:o5]
        gate_logits = z[..., o5:] + b_gate[i]
        g_a = jax.nn.sigmoid(gate_logits[..., :D_MODEL])
        g_b = jax.nn.sigmoid(gate_logits[..., D_MODEL:])

        a = a_val * jax.nn.sigmoid(a_gt)
        a = causal_dwconv(a, conv_a_w[i]) + conv_a_b[i]
        a = jax.nn.silu(layernorm(a, ln_a_g[i], ln_a_b[i]))
        y_a = jnp.einsum("bsc,cd->bsd", a, w_a_out[i])

        s = sc_b * causal_dwconv(sc_c * sc_v, conv_b_w[i])
        y_b = jnp.einsum("bsc,cd->bsd", s, w_b_out[i])

        x = x + jnp.einsum("bsd,de->bse", g_a * y_a + g_b * y_b, w_o[i])

        h = rmsnorm(x, g_ffn[i])
        u = jnp.einsum("bsd,df->bsf", h, w_up[i])
        f_gate = causal_dwconv(u[..., :D_FF], conv_f_w[i]) + conv_f_b[i]
        f = jax.nn.gelu(f_gate, approximate=True) * u[..., D_FF:]
        x = x + jnp.einsum("bsf,fd->bsd", f, w_down[i])

        pg = jax.nn.sigmoid(jnp.einsum("bsd,de->bse", rmsnorm(x, g_ple[i]), w_ple_gate[i]))
        x = x + pg * jnp.einsum("bsk,kd->bsd", p[i], w_ple[i])

    return rmsnorm(x, g_final)


GRID_W = 64
CTX_LEN = 256
D_MIX = D_MODEL
D_ATTN = D_MIX // 2
D_POOL = D_MIX - D_ATTN
MLA_HEADS = 4
QK_NOPE_DIM = 128
QK_ROPE_DIM = 64
QK_HEAD_DIM = QK_NOPE_DIM + QK_ROPE_DIM
V_HEAD_DIM = D_ATTN // MLA_HEADS
Q_LORA_RANK = 256
KV_LORA_RANK = 128
ROPE_AXIS_DIM = QK_ROPE_DIM // 2
ROPE_BASE = 10000.0
POOL_WINDOWS = (2, 4, 8, 16)
POOL_GROUPS = len(POOL_WINDOWS)
POOL_GROUP_DIM = D_POOL // POOL_GROUPS
Q_BLOCK = 128
NORM_EPS = 1e-6

OFF_CQ = 0
OFF_CKV = OFF_CQ + Q_LORA_RANK
OFF_KR = OFF_CKV + KV_LORA_RANK
OFF_GA = OFF_KR + QK_ROPE_DIM
OFF_PIN = OFF_GA + D_ATTN
OFF_GP = OFF_PIN + D_POOL
D_IN_PROJ = OFF_GP + D_POOL


def _rms(x, g):
    xf = x.astype(jnp.float32)
    y = xf * lax.rsqrt(jnp.mean(xf * xf, axis=-1, keepdims=True) + NORM_EPS)
    return (y * g.astype(jnp.float32)).astype(x.dtype)

def _rotate_half(x):
    x1, x2 = jnp.split(x, 2, axis=-1)
    return jnp.concatenate([-x2, x1], axis=-1)

def _axial_rope_tables(L):
    rows = L // GRID_W
    row = jnp.repeat(jnp.arange(rows, dtype=jnp.float32), GRID_W)
    col = jnp.tile(jnp.arange(GRID_W, dtype=jnp.float32), rows)
    n_freq = ROPE_AXIS_DIM // 2
    inv = ROPE_BASE ** (-jnp.arange(n_freq, dtype=jnp.float32) / n_freq)
    ang_r = row[:, None] * inv
    ang_c = col[:, None] * inv
    ang = jnp.concatenate([ang_r, ang_r, ang_c, ang_c], axis=-1)
    return jnp.cos(ang), jnp.sin(ang)

def _apply_axial_rope(x, cos, sin):
    xr, xc = jnp.split(x, 2, axis=-1)
    rot = jnp.concatenate([_rotate_half(xr), _rotate_half(xc)], axis=-1)
    c = cos[:, None, :]
    s = sin[:, None, :]
    return (x.astype(jnp.float32) * c + rot.astype(jnp.float32) * s).astype(x.dtype)

def _mla_qkv(u, q_lora_g, w_uq, kv_lora_g, w_ukv, q_norm_g, k_norm_g, rope):
    B, L = u.shape[0], u.shape[1]
    cq = u[..., OFF_CQ:OFF_CKV]
    ckv = u[..., OFF_CKV:OFF_KR]
    k_rope = u[..., OFF_KR:OFF_GA]
    q = (_rms(cq, q_lora_g) @ w_uq).reshape(B, L, MLA_HEADS, QK_HEAD_DIM)
    kv = (_rms(ckv, kv_lora_g) @ w_ukv).reshape(B, L, MLA_HEADS, QK_NOPE_DIM + V_HEAD_DIM)
    k_nope, v = kv[..., :QK_NOPE_DIM], kv[..., QK_NOPE_DIM:]
    k = jnp.concatenate(
        [k_nope, jnp.broadcast_to(k_rope[:, :, None, :], (B, L, MLA_HEADS, QK_ROPE_DIM))], axis=-1)
    q = _rms(q, q_norm_g)
    k = _rms(k, k_norm_g)
    if rope is not None:
        cos, sin = rope
        q = jnp.concatenate([q[..., :QK_NOPE_DIM], _apply_axial_rope(q[..., QK_NOPE_DIM:], cos, sin)], axis=-1)
        k = jnp.concatenate([k[..., :QK_NOPE_DIM], _apply_axial_rope(k[..., QK_NOPE_DIM:], cos, sin)], axis=-1)
    tr = lambda t: jnp.transpose(t, (0, 2, 1, 3))
    return tr(q), tr(k), tr(v)

def _attend(q, k, v):
    B, H, Lq, dk = q.shape
    nb = Lq // Q_BLOCK
    scale = QK_HEAD_DIM ** -0.5
    qb = jnp.transpose(q.reshape(B, H, nb, Q_BLOCK, dk), (2, 0, 1, 3, 4))

    def one(qblk):
        s = jnp.einsum('bhqd,bhkd->bhqk', qblk, k).astype(jnp.float32) * scale
        p = jax.nn.softmax(s, axis=-1)
        return jnp.einsum('bhqk,bhkd->bhqd', p.astype(v.dtype), v)

    o = lax.map(one, qb)
    o = jnp.transpose(o, (1, 3, 0, 2, 4)).reshape(B, Lq, H * v.shape[-1])
    return o

def _multiscale_pool(u, w_pool, pool_scale):
    B, L, _ = u.shape
    ug = u.reshape(B, L, POOL_GROUPS, POOL_GROUP_DIM)
    cs = jnp.concatenate(
        [jnp.zeros((B, 1, POOL_GROUPS, POOL_GROUP_DIM), jnp.float32),
         jnp.cumsum(ug.astype(jnp.float32), axis=1)], axis=1)
    t = jnp.arange(L, dtype=jnp.int32)[:, None]
    w = jnp.array(POOL_WINDOWS, dtype=jnp.int32)[None, :]
    lo = jnp.clip(t - w // 2, 0, L)
    hi = jnp.clip(t - w // 2 + w, 0, L)
    g = jnp.arange(POOL_GROUPS, dtype=jnp.int32)[None, :]
    win_sum = cs[:, hi, g, :] - cs[:, lo, g, :]
    cnt = (hi - lo).astype(jnp.float32)[None, :, :, None]
    pooled = (win_sum / cnt - ug.astype(jnp.float32)).astype(u.dtype)
    y = jnp.einsum('blgc,gcd->blgd', pooled, w_pool).reshape(B, L, D_POOL)
    return y * pool_scale

def _branches(u, mla_out, w_pool, pool_scale):
    gate_a = u[..., OFF_GA:OFF_PIN]
    pool_in = u[..., OFF_PIN:OFF_GP]
    gate_p = u[..., OFF_GP:D_IN_PROJ]
    br_a = jax.nn.silu(gate_a) * mla_out
    br_p = jax.nn.silu(gate_p) * _multiscale_pool(pool_in, w_pool, pool_scale)
    return jnp.concatenate([br_a, br_p], axis=-1)

def second_inputs(seed: int = 0) -> dict:
    key = jax.random.key(seed)
    ks = jax.random.split(key, 20)
    f32 = jnp.float32
    nrm = lambda k, shape, s: jax.random.normal(k, shape, f32) * s
    return {
        "x": nrm(ks[0], (BATCH, SEQ, D_MODEL), 1.0),
        "c": nrm(ks[1], (BATCH, D_MODEL), 1.0),
        "ctx": nrm(ks[2], (BATCH, CTX_LEN, D_MODEL), 1.0),
        "c_ctx": nrm(ks[3], (D_MODEL,), 1.0),
        "w_mod": nrm(ks[4], (DEPTH, D_MODEL, 3 * D_MODEL), 0.5 * D_MODEL ** -0.5),
        "b_mod": nrm(ks[5], (DEPTH, 3 * D_MODEL), 0.02),
        "norm_g": 1.0 + nrm(ks[6], (DEPTH, D_MODEL), 0.1),
        "w_in": nrm(ks[7], (DEPTH, D_MODEL, D_IN_PROJ), D_MODEL ** -0.5),
        "q_lora_g": 1.0 + nrm(ks[8], (DEPTH, Q_LORA_RANK), 0.1),
        "w_uq": nrm(ks[9], (DEPTH, Q_LORA_RANK, MLA_HEADS * QK_HEAD_DIM), Q_LORA_RANK ** -0.5),
        "kv_lora_g": 1.0 + nrm(ks[10], (DEPTH, KV_LORA_RANK), 0.1),
        "w_ukv": nrm(ks[11], (DEPTH, KV_LORA_RANK, MLA_HEADS * (QK_NOPE_DIM + V_HEAD_DIM)), KV_LORA_RANK ** -0.5),
        "q_norm_g": 1.0 + nrm(ks[12], (DEPTH, QK_HEAD_DIM), 0.1),
        "k_norm_g": 1.0 + nrm(ks[13], (DEPTH, QK_HEAD_DIM), 0.1),
        "w_pool": nrm(ks[14], (DEPTH, POOL_GROUPS, POOL_GROUP_DIM, POOL_GROUP_DIM), POOL_GROUP_DIM ** -0.5),
        "pool_scale": 1.0 + nrm(ks[15], (DEPTH, D_POOL), 0.1),
        "w_out": nrm(ks[16], (DEPTH, D_MIX, D_MODEL), D_MIX ** -0.5),
    }

def second_block(x, c, ctx, c_ctx, w_mod, b_mod, norm_g, w_in, q_lora_g, w_uq, kv_lora_g, w_ukv,
              q_norm_g, k_norm_g, w_pool, pool_scale, w_out):
    L = x.shape[1]
    rope = _axial_rope_tables(L)
    for l in range(DEPTH):
        mod = jax.nn.silu(c) @ w_mod[l] + b_mod[l]
        shift, scale, gate = jnp.split(mod, 3, axis=-1)
        mod_c = jax.nn.silu(c_ctx) @ w_mod[l] + b_mod[l]
        shift_c, scale_c, gate_c = jnp.split(mod_c, 3, axis=-1)

        h = _rms(x, norm_g[l]) * (1.0 + scale[:, None, :]) + shift[:, None, :]
        hc = _rms(ctx, norm_g[l]) * (1.0 + scale_c) + shift_c
        u = h @ w_in[l]
        uc = hc @ w_in[l]

        q, k, v = _mla_qkv(u, q_lora_g[l], w_uq[l], kv_lora_g[l], w_ukv[l],
                           q_norm_g[l], k_norm_g[l], rope)
        qc, kc, vc = _mla_qkv(uc, q_lora_g[l], w_uq[l], kv_lora_g[l], w_ukv[l],
                              q_norm_g[l], k_norm_g[l], None)
        k_all = jnp.concatenate([kc, k], axis=2)
        v_all = jnp.concatenate([vc, v], axis=2)
        attn = _attend(q, k_all, v_all)
        y = _branches(u, attn, w_pool[l], pool_scale[l]) @ w_out[l]
        x_new = x + gate[:, None, :] * y

        if l < DEPTH - 1:
            attn_c = _attend(qc, kc, vc)
            yc = _branches(uc, attn_c, w_pool[l], pool_scale[l]) @ w_out[l]
            ctx = ctx + gate_c * yc
        x = x_new
    return x


def setup_inputs(seed=0):
    out = dict(first_inputs(seed))
    for name, value in second_inputs(seed + 1).items():
        if name != "x":
            out[name + "_2"] = value
    return out


def reference(
    x, p, g_mix, w_in, b_gate, conv_a_w, conv_a_b, ln_a_g, ln_a_b, w_a_out, conv_b_w, w_b_out,
    w_o, g_ffn, w_up, conv_f_w, conv_f_b, w_down, g_ple, w_ple, w_ple_gate, g_final, c_2, ctx_2,
    c_ctx_2, w_mod_2, b_mod_2, norm_g_2, w_in_2, q_lora_g_2, w_uq_2, kv_lora_g_2, w_ukv_2,
    q_norm_g_2, k_norm_g_2, w_pool_2, pool_scale_2, w_out_2,
):
    x = first_block(
        x, p, g_mix, w_in, b_gate, conv_a_w, conv_a_b, ln_a_g, ln_a_b, w_a_out, conv_b_w,
        w_b_out, w_o, g_ffn, w_up, conv_f_w, conv_f_b, w_down, g_ple, w_ple, w_ple_gate,
        g_final,
    )
    return second_block(
        x, c_2, ctx_2, c_ctx_2, w_mod_2, b_mod_2, norm_g_2, w_in_2, q_lora_g_2, w_uq_2,
        kv_lora_g_2, w_ukv_2, q_norm_g_2, k_norm_g_2, w_pool_2, pool_scale_2, w_out_2,
    )


_drawn_inputs = setup_inputs


def setup_inputs(seed=0):
    import zlib

    import numpy as np

    out = dict(_drawn_inputs(seed))
    spreads = {}
    factors = {'b_gate': 8.0,
     'conv_a_b': 4.79,
     'ln_a_g': 3.21,
     'ln_a_b': 8.0,
     'conv_f_b': 6.214,
     'g_ple': 7.987,
     'ctx_2': 8.0,
     'c_ctx_2': 8.0,
     'b_mod_2': 5.488,
     'norm_g_2': 3.107,
     'q_lora_g_2': 8.0,
     'w_uq_2': 4.478,
     'kv_lora_g_2': 8.0,
     'q_norm_g_2': 8.0,
     'k_norm_g_2': 8.0,
     'pool_scale_2': 4.412}
    for name, (base, spread) in spreads.items():
        noise = np.random.default_rng([zlib.crc32(name.encode()), seed]).standard_normal(out[name].shape)
        drawn = base * np.exp(spread * noise) if base else spread * noise
        out[name] = __import__('jax').numpy.asarray(drawn.astype(out[name].dtype))
    for name, factor in factors.items():
        out[name] = (out[name] * factor).astype(out[name].dtype)
    return out
```

```python
import concourse.bass as bass
from concourse import mybir
from contextlib import ExitStack

F32 = mybir.dt.float32
F32R = mybir.dt.float32r
ALU = mybir.AluOpType
ACT = mybir.ActivationFunctionType
AX = mybir.AxisListType

P = 128
S = 1024
D = 1024
KD = D // P
H = 512
DC = 512
KC = DC // P
TAPS_A, TAPS_B, TAPS_F = 31, 3, 3
DFF = 2816
NF = DFF // P
FC = 2
NCH = NF // FC
PLE = 256
CTX = 256
NKEY = S + CTX
KT = NKEY // P
HEADS, NOPE, ROPE, VD = 4, 128, 64, 128
QH = NOPE + ROPE
EPS = 1e-6
SCALE = QH ** -0.5
WINDOWS = (2, 4, 8, 16)
IN2 = 1984
OFF_CKV, OFF_KR, OFF_GA, OFF_PIN, OFF_GP = 256, 384, 448, 960, 1472

ROWS = [
    [("conv_a_w", 124), ("conv_a_b", 4)],
    [("b_gate", 16), ("ln_a_g", 4), ("ln_a_b", 4), ("conv_b_w", 12), ("g_ffn", 8), ("conv_f_b", 22),
     ("g_ple", 8), ("g_final", 8), ("norm_g_2", 8), ("b_mod_2", 24), ("q_lora_g_2", 2),
     ("kv_lora_g_2", 1), ("pool_scale_2", 4), ("q_norm_g_2", 2), ("k_norm_g_2", 2)],
    [("conv_f_w", 66), ("c_2", 8), ("c_ctx_2", 8)],
]
COL = {}
for _b, _bin in enumerate(ROWS):
    _at = _b * P
    for _name, _n in _bin:
        COL[_name] = _at
        _at += _n

SLABS = {}
_at = 0
for _name, _n in (("glu", 2 * KC), ("short", 3 * KC), ("mix_b", 2 * KD), ("mix_a", 2 * KD), ("wo", KD),
                  ("ffn", 6), ("ffn_loop", 8 * (NCH - 1)), ("ffn_end", 4), ("ple", 2 * KD), ("ga", 4), ("mla_in", 4),
                  ("pin", 4), ("pool", 8), ("heads", 2 * HEADS), ("out", KD), ("end", 0)):
    SLABS[_name] = _at
    _at += _n
JOBS = {}
_at = 0
for _name, _n in (("x", 8), ("glu", 2 * KC), ("short", 3 * KC), ("mix_b", 2 * KD), ("mix_a", 2 * KD), ("wo", KD),
                  ("ctx", 2), ("p", 2), ("ffn", 4), ("ffn_loop", 12 * (NCH - 1)), ("ffn_end", 8),
                  ("ple", 2 * KD), ("ga", 4), ("mla_in", 6), ("pin", 4), ("pool", 8), ("heads", 6 * HEADS),
                  ("out", KD), ("end", 0)):
    JOBS[_name] = _at
    _at += _n


class Lin:

    def __init__(self, c, n=0, i=0):
        self.c, self.n, self.i = c, n, i

    def __add__(self, k):
        return Lin(self.c + k, self.n, self.i)

    def val(self, k=0):
        return self.c + k + self.n * self.i if self.n else self.c + k

    def half(self):
        return self.c // 2 + (self.n // 2) * self.i if self.n else self.c // 2

    @property
    def slot(self):
        assert self.n % 2 == 0
        return self.c % 2


N_ROW_DMAS = sum(len(b) for b in ROWS) + 2


def ds(i, n=1):
    return bass.ds(i, n)


def build_program(nc, A, out, ydram):
    KB4 = 4096
    TB = 4160

    def at(name, shape, dtype, offset):
        return nc.alloc_sbuf_tensor_at(name, shape, dtype, offset=offset)

    o_raw = 16512
    o_whi = o_raw + 2 * KB4
    o_wlo = o_whi + 2 * KB4
    o_xah = o_wlo + 2 * KB4
    o_xal = o_xah + 8 * KB4
    o_xbh = o_xal + 8 * KB4
    o_xbl = o_xbh + 8 * KB4
    o_r = o_xbl + 8 * KB4
    o_c = o_r + 8 * KB4
    o_t = o_c + 3648
    o_rbc = o_t + 4 * TB
    assert o_rbc + KB4 <= nc.sbuf_usable_end
    raw = at("raw", [P, 2, 1024], F32, o_raw)
    whi = at("whi", [P, 2, 1024], F32R, o_whi)
    wlo = at("wlo", [P, 2, 1024], F32R, o_wlo)
    XAh = at("xa_hi", [P, 8, S], F32R, o_xah)
    XAl = at("xa_lo", [P, 8, S], F32R, o_xal)
    XBh = at("xb_hi", [P, 8, S], F32R, o_xbh)
    XBl = at("xb_lo", [P, 8, S], F32R, o_xbl)
    R = at("resid", [P, 8, S], F32, o_r)
    ident = at("ident", [P, P], F32, o_c)
    ones = at("ones", [P, P], F32, o_c + 512)
    tab = at("tab", [P, 3 * P], F32, o_c + 1024)
    small = at("small", [P, 128], F32, o_c + 2560)
    cs_hi = at("cs_hi", [P, KD, 2], F32R, o_c + 3072)
    cs_lo = at("cs_lo", [P, KD, 2], F32R, o_c + 3136)
    mod_sb = at("mod_sb", [P, 24, 2], F32, o_c + 3200)
    rotm = at("rotm", [ROPE, ROPE], F32, o_c + 3392)
    T = [at(f"t{k}", [P, TB // 4], F32, o_t + k * TB) for k in range(4)]
    rbc = at("rbc", [P, S], F32, o_rbc)
    xn = at("x_nat", [P, 2, D], F32, o_r)
    gbc = at("g_mix_bc", [P, D], F32, o_r + 2 * KB4)
    xs = at("x_scaled", [P, 2, D], F32, o_r + 3 * KB4)
    sqj = at("sq_junk", [P, D], F32, o_r + 5 * KB4)
    rows = at("rows", [P, 3, P], F32, o_r + 6 * KB4)
    LPAD = TAPS_A - 1
    gpad = at("glu_pad", [P, KC, S + LPAD + 2], F32, o_r)
    conv = at("conv_a", [P, KC, S], F32, o_xbl)
    cstage = at("ctx_nat", [P, 2, D], F32, o_xah + 4 * KB4)
    pstage = at("p_nat", [P, 8, PLE], F32, o_xah + 6 * KB4)
    ctxT = at("ctx_t", [P, KD, CTX], F32, o_xal + 6 * KB4)
    hch = at("hc_hi", [P, KD, CTX], F32R, o_xah + 6 * KB4)
    hcl = at("hc_lo", [P, KD, CTX], F32R, o_xal + 6 * KB4)
    S1 = at("sum_sq", [P, S], F32, o_xah)
    S2 = at("sum_sq_g", [P, S], F32, o_xah + KB4)
    Q1 = at("sq", [P, S], F32, o_xah + 2 * KB4)
    Q2 = at("sq_g", [P, S], F32, o_xah + 3 * KB4)
    ga = at("silu_gate_a", [P, HEADS, S], F32, o_xal)
    cosb = at("cosb", [ROPE, S], F32, o_xah)
    sinb = at("sinb", [ROPE, S], F32, o_xah + KB4)
    sqck = at("sq_ckv", [P, NKEY], F32, o_xah + 2 * KB4)
    dgck = at("diag_ckv", [P, KT, P], F32, o_xah + 2 * KB4)
    CKh = at("ck_hi", [P, NKEY], F32R, o_r)
    CKl = at("ck_lo", [P, NKEY], F32R, o_r + 5120)
    CQh = at("cq_hi", [P, 2, S], F32R, o_r + 10240)
    CQl = at("cq_lo", [P, 2, S], F32R, o_r + 18432)
    krot = at("k_rot", [ROPE, NKEY], F32, o_r + 26624)
    ckvT = at("ckv_t", [P, NKEY], F32, o_t)
    krT = at("kr_t", [ROPE, NKEY], F32, o_t + 5120)
    sqkr = at("sq_kr", [ROPE, NKEY], F32, o_t + 10240)
    U3 = at("u3", [P, NKEY], F32, o_t + 15360)
    upad = at("u_pad", [P, TB // 4], F32, o_xah)
    wA = at("win_a", [P, TB // 4], F32, o_xah + TB)
    wB = at("win_b", [P, TB // 4], F32, o_xah + 2 * TB)
    inv = at("inv_cnt", [P, S], F32, o_t + 5120)
    pl = at("pooled", [P, S], F32, o_t)
    sgp = at("silu_gate_p", [P, S], F32, o_t + 5120)
    QNh = at("qn_hi", [P, S], F32R, o_xbh)
    QNl = at("qn_lo", [P, S], F32R, o_xbh + 4096)
    QRh = at("qr_hi", [ROPE, S], F32R, o_xbh + 8192)
    QRl = at("qr_lo", [ROPE, S], F32R, o_xbh + 12288)
    KNh = at("kn_hi", [P, NKEY], F32R, o_xbh + 16384)
    KNl = at("kn_lo", [P, NKEY], F32R, o_xbh + 21504)
    KRh = at("kr_hi", [ROPE, NKEY], F32R, o_xbh + 26624)
    KRl = at("kr_lo", [ROPE, NKEY], F32R, o_xbh + 31744)
    Vh = at("v_hi", [P, KT, VD], F32R, o_xbh + 36864)
    Vl = at("v_lo", [P, KT, VD], F32R, o_xbh + 41984)
    Pr = [at(f"prob{k}", [P, NKEY], F32, o_xbh + 47104 + 5120 * k) for k in range(2)]
    cosq = at("cosq", [ROPE, S], F32, o_xbh + 57344)
    sinq = at("sinq", [ROPE, S], F32, o_xbh + 61440)
    PTh = at("pt_hi", [P, KT, 2 * P], F32R, o_xah)
    PTl = at("pt_lo", [P, KT, 2 * P], F32R, o_t)
    dgp = at("diag_p", [P, 2, P], F32, o_xah + KT * 2 * P * 4)
    dgh = at("diag_h", [P, KT, P], F32, o_t)
    rb_h = at("rbc_h", [P, NKEY], F32, o_t + 5120)
    ybuf = at("y_back", [P, 8, S], F32, o_xbh)
    yout = at("out_t", [P, 2, S], F32, o_xbl)
    onat = at("out_nat", [P, 2, 8, P], F32, o_xbl + 2 * KB4)
    PS = nc.alloc_psum_tensor("ps", [P, 4096], F32)
    ST, SC = 2048, 3584

    sems = {}

    def sem(name):
        if name not in sems:
            sems[name] = nc.alloc_semaphore(name)
        return sems[name]

    def pair(job, a=0, b=1024, p=P):
        return PS[0:p, 1024 * job.slot + a:1024 * job.slot + b]

    def f32(ap):
        return ap.bitcast(F32)

    def col(name, k, p=P):
        return tab[0:p, COL[name] + k:COL[name] + k + 1]

    def dcol(name, k):
        return tab[:, ds(k + COL[name])]

    def tile(x, k, a=0, b=1024):
        if isinstance(k, int):
            return x[:, k, a:b]
        return x[:, ds(k), a:b].rearrange("p o n -> p (o n)")

    raw_in = [sem("raw_in0"), sem("raw_in1")]
    pair_free = [sem("pair_free0"), sem("pair_free1")]
    job_done, split_done, slab_begun = sem("job_done"), sem("split_done"), sem("slab_begun")

    def free(job):
        return pair_free[job.slot], job.half() + 1

    def settle(engine):
        engine.wait_ge(sem("ident_in"), 16)

    def sync_program(sp):
        def load(slab, dst_cols, src, first=False):
            if not first:
                sp.wait_ge(split_done, slab.val(-1))
            sp.dma_start(dst_cols, src).then_inc(raw_in[slab.slot], 16)

        def slab8(slab, w, c, first=False):
            load(slab, raw[:, slab.slot, :].rearrange("p (k n) -> p k n", n=P),
                 w[:, ds(c, P)].rearrange("(k p) n -> p k n", p=P), first)

        def slabk(slab, w, kts, c, n=P, r0=0):
            load(slab, raw[:, slab.slot, 0:kts * n].rearrange("p (k n) -> p k n", n=n),
                 w[ds(r0, kts * P), ds(c, n)].rearrange("(k p) n -> p k n", p=P))

        w_in, w_up, w_down = A["w_in"][0], A["w_up"][0], A["w_down"][0]
        L = Lin(SLABS["glu"])
        sp.dma_start(xn[:, 0, :], A["x"][0, 0:P, :]).then_inc(sem("x_in0"), 16)
        sp.dma_start(gbc[:, :], A["g_mix"][0:1, :].to_broadcast([P, D])).then_inc(sem("g_in"), 16)
        sp.dma_start(xn[:, 1, :], A["x"][0, P:2 * P, :]).then_inc(sem("x_in1"), 16)
        slab8(L, w_in, 0, True)
        slab8(L + 1, w_in, DC, True)
        for t in range(2, 8):
            sp.wait_ge(sem("xs_ready"), t - 1)
            sp.dma_start(xn[:, t % 2, :], A["x"][0, t * P:(t + 1) * P, :]).then_inc(sem(f"x_in{t % 2}"), 16)
        with sp.Fori(1, KC) as i:
            L = Lin(SLABS["glu"], 2, i)
            slab8(L, w_in, i * P)
            slab8(L + 1, w_in, i * P + DC)
        with sp.Fori(0, 2) as q:
            for u in range(2):
                L = Lin(SLABS["short"] + 3 * u, 6, q)
                for k, c in enumerate((1536, 2048, 1024)):
                    slab8(L + k, w_in, q * (2 * P) + (c + u * P))
        for name, c, w2 in (("mix_b", 3584, A["w_b_out"][0]), ("mix_a", 2560, A["w_a_out"][0])):
            with sp.Fori(1, KD + 1) as m:
                L = Lin(SLABS[name] - 2, 2, m)
                slab8(L, w_in, m * P + (c - P))
                slabk(L + 1, w2, KC, m * P - P)
        sp.wait_ge(sem("mix_done"), 8)

        def x_columns(u, c):
            sp.dma_start(T[1 + u][:, 0:1024].rearrange("p (t f) -> p t f", f=P),
                         A["x"][0, :, ds(c, P)].rearrange("(t p) f -> p t f", p=P)).then_inc(sem(f"xc_in{u}"), 16)

        for u in range(2):
            slab8(Lin(SLABS["wo"] + u), A["w_o"][0], u * P)
            x_columns(u, u * P)
        with sp.Fori(1, KD // 2) as q:
            for u in range(2):
                slab8(Lin(SLABS["wo"] + u, 2, q), A["w_o"][0], q * (2 * P) + u * P)
                sp.wait_ge(sem("xt_pe"), q * 2 + (u - 1))
                x_columns(u, q * (2 * P) + u * P)
        sp.wait_ge(job_done, JOBS["ctx"])
        sp.dma_start(cstage[:, :, :], A["ctx_2"][0].rearrange("(t p) f -> p t f", p=P)).then_inc(sem("ctx_p_in"), 16)
        sp.dma_start(pstage[:, :, :], A["p"][0, 0].rearrange("(t p) f -> p t f", p=P)).then_inc(sem("ctx_p_in"), 16)

        def up_slabs(L, c):
            for k, off in enumerate((0, DFF, P, P + DFF)):
                slab8(L + k, w_up, c * (2 * P) + off)
            for k in range(2):
                slab8(L + 4 + k, A["w_mod_2"][0], c * (2 * P) + k * P)

        def down_slabs(L, c):
            for k in range(2):
                slabk(L + k, w_down, FC, k * H, H, c * (2 * P))

        up_slabs(Lin(SLABS["ffn"]), 0)
        with sp.Fori(0, (NCH - 1) // 2) as q:
            for u in range(2):
                L = Lin(SLABS["ffn_loop"] + 8 * u, 16, q)
                up_slabs(L, q * 2 + (1 + u))
                down_slabs(L + 6, q * 2 + u)
        L = Lin(SLABS["ffn_end"])
        down_slabs(L, NCH - 1)
        for k in range(2):
            slab8(L + 2 + k, A["w_mod_2"][0], (2 * NCH + k) * P)
        with sp.Fori(0, KD) as m:
            L = Lin(SLABS["ple"], 2, m)
            slabk(L, A["w_ple"][0], 2, m * P)
            slab8(L + 1, A["w_ple_gate"][0], m * P)
        w2 = A["w_in_2"][0]
        L = Lin(SLABS["ga"])
        for i in range(4):
            slab8(L + i, w2, OFF_GA + i * P)
        sp.wait_ge(sem("rf_bc"), 1)
        sp.dma_start(cosb[:, :], A["rope_cos"]).then_inc(sem("rope_in"), 16)
        sp.dma_start(sinb[:, :], A["rope_sin"]).then_inc(sem("rope_in"), 16)
        for m in range(8):
            sp.wait_ge(sem("y_ready"), m + 1)
            sp.dma_start(ydram[m], R[:, m, :]).then_inc(sem("y_out"), 16)
        L = Lin(SLABS["mla_in"])
        for k, c in enumerate((OFF_CKV, OFF_KR, 0, P)):
            slab8(L + k, w2, c)
        L = Lin(SLABS["pin"])
        for gq in range(4):
            slab8(L + gq, w2, OFF_PIN + gq * P)
        L = Lin(SLABS["pool"])
        for gq in range(4):
            slabk(L + 2 * gq, A["w_pool_2"][0, gq], 1, 0)
            slab8(L + 2 * gq + 1, w2, OFF_GP + gq * P)
        sp.wait_ge(job_done, JOBS["heads"])
        sp.dma_start(cosq[:, :], A["rope_cos"]).then_inc(sem("rope_in"), 16)
        sp.dma_start(sinq[:, :], A["rope_sin"]).then_inc(sem("rope_in"), 16)
        with sp.Fori(0, HEADS) as h:
            L = Lin(SLABS["heads"], 2, h)
            slabk(L, A["w_uq_2"][0], 2, h * QH, QH)
            slabk(L + 1, A["w_ukv_2"][0], 1, h * (NOPE + VD), NOPE + VD)
        L = Lin(SLABS["out"])
        slab8(L, A["w_out_2"][0], 0)
        slab8(L + 1, A["w_out_2"][0], P)
        sp.wait_ge(sem("y_out"), 8 * 16)
        sp.wait_ge(sem("pv_done"), 4 * HEADS)
        for m in range(8):
            sp.dma_start(ybuf[:, m, :], ydram[m]).then_inc(sem("y_in"), 16)
        for m in range(2, 8):
            slab8(L + m, A["w_out_2"][0], m * P)
        for m in range(8):
            sp.wait_ge(sem("on_ready"), m + 1)
            sp.dma_start(out[0, :, m * P:(m + 1) * P].rearrange("(t p) f -> p t f", p=P),
                         onat[:, m % 2, :, :]).then_inc(sem(f"out_done{m % 2}"), 16)
        for k in range(2):
            sp.wait_ge(sem(f"out_done{k}"), 4 * 16)

    def pool_program(pool, n_slabs):
        def split(slab, first=False):
            pool.wait_ge(raw_in[slab.slot], (slab.half() + 1) * 16)
            if not first:
                pool.wait_ge(slab_begun, slab.val())
            nc.gpsimd.tensor_tensor(small[:, 30 + slab.slot:31 + slab.slot], ones[:, 0:1], ones[:, 0:1], ALU.mult)
            nc.gpsimd.tensor_scalar(whi[:, slab.slot, :], raw[:, slab.slot, :], 1.0, 0.0,
                                    ALU.mult, ALU.add).then_inc(sem("split_hi"), 1)
            pool.wait_ge(sem("split_hi"), slab.val(1))
            nc.gpsimd.tensor_tensor(wlo[:, slab.slot, :], raw[:, slab.slot, :], f32(whi[:, slab.slot, :]),
                                    ALU.subtract).then_inc(split_done, 1)

        pool.wait_ge(sem("ones_set"), 1)
        split(Lin(0), True)
        split(Lin(1), True)
        with pool.Fori(1, n_slabs // 2) as q:
            split(Lin(0, 2, q))
            split(Lin(1, 2, q))
        if n_slabs % 2:
            split(Lin(n_slabs - 1))

    def tensor_program(pe):
        mm = nc.tensor.matmul

        def split_products(dst, whk, wlk, rhk, rlk, first, last, begun=None):
            n = len(dst)
            done = None
            for w, r, f, l in ((whk, rhk, True, False), (whk, rlk, False, False), (wlk, rhk, False, True)):
                for j in range(n):
                    ins = mm(dst[j], w, r[j], start=first and f, stop=last and l)
                    if begun is not None:
                        ins.then_inc(begun, 1)
                        begun = None
                    done = ins
            return done

        def gemm(job, slab, rh, rl, kts, wcol, new_slab=True, n=1024, each_k=None, waited=KD, order=None,
                 col0=0, p=P):
            if job.n or job.c >= 2:
                pe.wait_ge(pair_free[job.slot], job.half())
            if new_slab:
                pe.wait_ge(split_done, slab.val(1))
            cuts = [(a, min(a + H, n)) for a in range(0, n, H)]
            order = order or range(kts)
            for k in order:
                if each_k is not None and k < waited:
                    pe.wait_ge(each_k, k + 1)
                w = slice(wcol(k), wcol(k) + P)
                last = split_products(
                    [pair(job, a, b) for a, b in cuts], whi[0:p, slab.slot, w], wlo[0:p, slab.slot, w],
                    [rh[0:p, k, col0 + a:col0 + b] for a, b in cuts],
                    [rl[0:p, k, col0 + a:col0 + b] for a, b in cuts],
                    k == order[0], k == order[-1], slab_begun if new_slab and k == order[0] else None)
            last.then_inc(job_done, 1)

        def w8(k):
            return k * P

        def transposes(job, srcs):
            if job.n or job.c >= 2:
                pe.wait_ge(pair_free[job.slot], job.half())
            for j, src in enumerate(srcs):
                last = nc.tensor.transpose(pair(job, j * P, j * P + P), src, ident[:, :])
            last.then_inc(job_done, 1)

        def column_sums(src, n, at_col, ready, count):
            pe.wait_ge(ready, count)
            for t in range(n):
                last = mm(PS[:, SC + at_col + t:SC + at_col + t + 1], src[:, t * P:(t + 1) * P],
                          ones[:, 0:1], start=True, stop=True)
            last.then_inc(sem("cols_pe"), 1)

        def broadcast(dg, n, count):
            pe.wait_ge(sem("diag"), count)
            d = dg.rearrange("p t n -> p (t n)")
            for a in range(0, n * P, H):
                b = min(a + H, n * P)
                last = mm(PS[:, ST + a:ST + b], ones[:, :], d[:, a:b], start=True, stop=True)
            last.then_inc(sem("bc_pe"), 1)

        pe.wait_ge(sem("ident_in"), 16)
        pe.wait_ge(sem("rotm_in"), 16)
        for t in range(8):
            pe.wait_ge(sem("xs_ready"), t + 1)
            transposes(Lin(JOBS["x"] + t), [xs[:, t % 2, k * P:(k + 1) * P] for k in range(KD)])
        pe.wait_ge(sem("rows_in"), N_ROW_DMAS * 16)
        for b in range(3):
            last = nc.tensor.transpose(PS[:, ST + b * P:ST + (b + 1) * P], rows[:, b, :], ident[:, :])
        last.then_inc(sem("tab_pe"), 1)
        pe.wait_ge(pair_free[0], 4)
        pe.wait_ge(pair_free[1], 4)
        with pe.Fori(0, KC) as i:
            J, L = Lin(JOBS["glu"], 2, i), Lin(SLABS["glu"], 2, i)
            gemm(J, L, XAh, XAl, KD, w8)
            gemm(J + 1, L + 1, XAh, XAl, KD, w8)
        with pe.Fori(0, 2) as q:
            for k in range(6):
                gemm(Lin(JOBS["short"] + k, 6, q), Lin(SLABS["short"] + k, 6, q), XAh, XAl, KD, w8)

        def mix_turns(name, rh, rl, a, b):
            with pe.Fori(a, b) as m:
                J, L = Lin(JOBS[name], 2, m), Lin(SLABS[name], 2, m)
                gemm(J, L, XAh, XAl, KD, w8)
                gemm(J + 1, L + 1, rh, rl, KC, w8)

        pe.wait_ge(sem("branch_lo"), 4)
        mix_turns("mix_b", XBh[:, 4:8, :], XBl[:, 4:8, :], 0, 2)
        pe.wait_ge(sem("ln_v"), 3)
        for a in (0, H):
            last = mm(PS[:, ST + a:ST + a + H], ones[:, :], T[1][:, a:a + H], start=True, stop=True)
        last.then_inc(sem("ln_pe"), 1)
        mix_turns("mix_b", XBh[:, 4:8, :], XBl[:, 4:8, :], 2, 4)
        column_sums(T[1], 8, 0, sem("ln_v"), 10)
        mix_turns("mix_b", XBh[:, 4:8, :], XBl[:, 4:8, :], 4, 6)
        broadcast(T[2][:, 0:1024].rearrange("p (t n) -> p t n", n=P), 8, 1)
        mix_turns("mix_b", XBh[:, 4:8, :], XBl[:, 4:8, :], 6, 8)
        pe.wait_ge(sem("branch_lo"), 8)
        mix_turns("mix_a", XBh[:, 0:4, :], XBl[:, 0:4, :], 0, 8)

        def wo_job(J, L, m, u, each_k=None):
            pe.wait_ge(sem(f"xc_in{u}"), (m // 2 if isinstance(m, int) else m[0]) * 16 + 16)
            if isinstance(m, tuple) or m >= 1:
                pe.wait_ge(sem("xt_sb"), m if isinstance(m, int) else m[1])
            for t in range(8):
                last = nc.tensor.transpose(PS[:, ST + t * P:ST + (t + 1) * P], T[1 + u][:, t * P:(t + 1) * P], ident[:, :])
            last.then_inc(sem("xt_pe"), 1)
            gemm(J, L, XAh, XAl, KD, w8, each_k=each_k)

        for m in range(2):
            wo_job(Lin(JOBS["wo"] + m), Lin(SLABS["wo"] + m), m, m, sem("mx_lo") if m == 0 else None)
        with pe.Fori(1, KD // 2) as q:
            for u in range(2):
                wo_job(Lin(JOBS["wo"] + u, 2, q), Lin(SLABS["wo"] + u, 2, q), (q, q * 2 + u), u)
        for t in range(2):
            pe.wait_ge(sem("cs_ready"), t + 1)
            transposes(Lin(JOBS["ctx"] + t), [cstage[:, t, k * P:(k + 1) * P] for k in range(KD)])
        for k in range(2):
            pe.wait_ge(sem("ctx_p_in"), 32)
            transposes(Lin(JOBS["p"] + k), [pstage[:, t, k * P:(k + 1) * P] for t in range(8)])

        def mod_slab(L, k, count):
            if count is not None:
                pe.wait_ge(sem("mod_read"), count)
            pe.wait_ge(split_done, L.val(1))
            for j in range(KD):
                w = slice(j * P, j * P + P)
                last = split_products([PS[:, SC + 64 + 2 * k:SC + 66 + 2 * k]], whi[:, L.slot, w], wlo[:, L.slot, w],
                                      [cs_hi[:, j, :]], [cs_lo[:, j, :]], j == 0, j == KD - 1,
                                      slab_begun if j == 0 else None)
            last.then_inc(sem("mod_pe"), 1)

        def ffn_down(J, L, slot):
            for m in range(KD):
                gemm(J + m, L + m // 4, XAh[:, 2 * slot:2 * slot + 2, :], XAl[:, 2 * slot:2 * slot + 2, :], FC,
                     lambda k: k * H + (m % 4) * P, new_slab=m % 4 == 0)

        J, L = Lin(JOBS["ffn"]), Lin(SLABS["ffn"])
        pe.wait_ge(sem("fx_lo"), 8)
        for k in range(2):
            gemm(J + k, L + k, XBh, XBl, KD, w8)
        column_sums(rbc, 8, 0, sem("ss_done"), 9)
        broadcast(T[3][:, 0:1024].rearrange("p (t n) -> p t n", n=P), 8, 2)
        for k in range(2, 4):
            gemm(J + k, L + k, XBh, XBl, KD, w8)
        pe.wait_ge(sem("cs_lo"), 1)
        mod_slab(L + 4, 0, None)
        mod_slab(L + 5, 1, None)
        with pe.Fori(0, (NCH - 1) // 2) as q:
            for u in range(2):
                J, L = Lin(JOBS["ffn_loop"] + 12 * u, 24, q), Lin(SLABS["ffn_loop"] + 8 * u, 16, q)
                for k in range(4):
                    gemm(J + k, L + k, XBh, XBl, KD, w8)
                mod_slab(L + 4, 0, q * 2 + (u + 1))
                mod_slab(L + 5, 1, None)
                pe.wait_ge(sem("f_lo"), q * 4 + (2 * u + 2))
                ffn_down(J + 4, L + 6, u)
        J, L = Lin(JOBS["ffn_end"]), Lin(SLABS["ffn_end"])
        pe.wait_ge(sem("f_lo"), 2 * NCH)
        ffn_down(J, L, (NCH - 1) % 2)
        mod_slab(L + 2, 0, NCH)
        mod_slab(L + 3, 1, None)

        def ple_pair(m, wait_k=None):
            J, L = Lin(JOBS["ple"], 2, m) if not isinstance(m, int) else Lin(JOBS["ple"] + 2 * m), \
                Lin(SLABS["ple"], 2, m) if not isinstance(m, int) else Lin(SLABS["ple"] + 2 * m)
            gemm(J, L, XAh[:, 4:6, :], XAl[:, 4:6, :], 2, w8)
            gemm(J + 1, L + 1, XBh, XBl, KD, w8, each_k=wait_k)

        ple_pair(0, sem("gx_lo"))
        pe.wait_ge(sem("mod_read"), NCH + 1)
        column_sums(rbc, 8, 0, sem("ss_done"), 17)
        broadcast(T[3][:, 0:1024].rearrange("p (t n) -> p t n", n=P), 8, 3)
        with pe.Fori(1, KD) as m:
            ple_pair(m)
        column_sums(S1, 8, 0, sem("s12_done"), 18)
        column_sums(S2, 8, 8, sem("s12_done"), 18)
        broadcast(Q1[:, :].rearrange("p (t n) -> p t n", n=P), 8, 4)
        pe.wait_ge(sem("rh_bc"), 1)
        broadcast(Q2[:, :].rearrange("p (t n) -> p t n", n=P), 8, 5)
        J, L = Lin(JOBS["ga"]), Lin(SLABS["ga"])
        for i in range(4):
            gemm(J + i, L + i, XBh, XBl, KD, w8, each_k=sem("h_lo") if i == 0 else None)
        J, L = Lin(JOBS["mla_in"]), Lin(SLABS["mla_in"])
        pe.wait_ge(sem("h_lo"), 9)
        for k in range(2):
            gemm(J + 2 * k, L + k, XBh, XBl, KD, w8)
            gemm(J + (2 * k + 1), L + k, hch, hcl, KD, w8, new_slab=False, n=CTX)
        for k in range(2):
            gemm(J + (4 + k), L + (2 + k), XBh, XBl, KD, w8)
        pe.wait_ge(sem("kr_sb"), 2)
        for a in (0, H):
            last = mm(PS[0:ROPE, ST + a:ST + a + H], rotm[:, :], krT[:, a:a + H], start=True, stop=True)
        last.then_inc(sem("rot_pe"), 1)
        column_sums(sqck, KT, 0, sem("ck_sq"), 2)
        J, L = Lin(JOBS["pin"]), Lin(SLABS["pin"])
        gemm(J, L, XBh, XBl, KD, w8)
        pe.wait_ge(sem("krot_mul"), 1)
        broadcast(dgck[:, :, :], KT, 6)
        column_sums(cqs[:, 0, :], 8, 16, sem("cq_ss"), 1)
        for gq in range(1, 4):
            gemm(J + gq, L + gq, XBh, XBl, KD, w8)
        J, L = Lin(JOBS["pool"]), Lin(SLABS["pool"])
        for gq in range(4):
            pe.wait_ge(sem("pool_lo"), gq + 1)
            gemm(J + 2 * gq, L + 2 * gq, XAh[:, 4 + gq:5 + gq, :], XAl[:, 4 + gq:5 + gq, :], 1, w8)
            gemm(J + (2 * gq + 1), L + (2 * gq + 1), XBh, XBl, KD, w8)

        CKh3, CKl3 = CKh[:, :].unsqueeze(1), CKl[:, :].unsqueeze(1)
        pe.wait_ge(sem("ck_lo"), 1)
        pe.wait_ge(sem("cq_lo"), 2)
        with pe.Fori(0, HEADS) as h:
            J, L = Lin(JOBS["heads"], 6, h), Lin(SLABS["heads"], 2, h)
            gemm(J, L, CQh, CQl, 2, lambda k: k * QH)
            gemm(J + 1, L, CQh, CQl, 2, lambda k: k * QH + NOPE, new_slab=False)
            gemm(J + 2, L + 1, CKh3, CKl3, 1, w8)
            gemm(J + 3, L + 1, CKh3, CKl3, 1, w8, new_slab=False, n=CTX, col0=S)
            pe.wait_ge(sem("ksq"), h + 1)
            pe.wait_ge(sem("qr_sb"), h + 1)
            for t in range(KT):
                last = mm(PS[:, SC + t:SC + t + 1], Pr[0][:, t * P:(t + 1) * P], ones[:, 0:1], start=True, stop=True)
            last.then_inc(sem("kcols"), 1)
            for a in (0, H):
                last = mm(PS[0:ROPE, ST + a:ST + a + H], rotm[:, :], U3[0:ROPE, a:a + H], start=True, stop=True)
            last.then_inc(sem("qrot_pe"), 1)
            pe.wait_ge(sem("kdiag"), h + 1)
            pe.wait_ge(sem("qr_lo"), h + 1)
            d = dgh[:, :, :].rearrange("p t n -> p (t n)")
            for a in range(0, NKEY, H):
                b = min(a + H, NKEY)
                last = mm(PS[:, ST + a:ST + b], ones[:, :], d[:, a:b], start=True, stop=True)
            last.then_inc(sem("kbc"), 1)
            pe.wait_ge(sem("qsq"), h + 1)
            for t in range(8):
                last = mm(PS[:, SC + 16 + t:SC + 17 + t], Pr[1][:, t * P:(t + 1) * P], ones[:, 0:1], start=True, stop=True)
            last.then_inc(sem("qcols"), 1)
            wv = slice(NOPE, NOPE + VD)
            for job, t0, t1 in ((J + 4, 0, 8), (J + 5, 8, KT)):
                pe.wait_ge(pair_free[job.slot], job.half())
                for t in range(t0, t1):
                    k = slice(t * P, (t + 1) * P)
                    o = pair(job, (t - t0) * P, (t - t0 + 1) * P)
                    mm(o, CKh[:, k], whi[:, (L + 1).slot, wv], start=True, stop=False)
                    mm(o, CKh[:, k], wlo[:, (L + 1).slot, wv], start=False, stop=False)
                    last = mm(o, CKl[:, k], whi[:, (L + 1).slot, wv], start=False, stop=True)
                last.then_inc(job_done, 1)
            pe.wait_ge(sem("kr_lo"), h + 1)
            pe.wait_ge(sem("v_lo"), h * 2 + 2)

            def scores(t):
                if t >= 2:
                    pe.wait_ge(sem("pt_lo"), h * 24 + 3 * (t - 1))
                q = slice(t * P, (t + 1) * P)
                terms = ((QNh, KNh), (QNh, KNl), (QNl, KNh), (QRh, KRh), (QRh, KRl), (QRl, KRh))
                for n_, (ql, kr_) in enumerate(terms):
                    for c0 in range(0, NKEY, H):
                        c1 = min(c0 + H, NKEY)
                        last = mm(PS[:, 1536 * (t % 2) + c0:1536 * (t % 2) + c1], ql[:, q], kr_[:, c0:c1],
                                  start=n_ == 0, stop=n_ == 5)
                last.then_inc(sem("s_done"), 1)

            scores(0)
            scores(1)
            for g in range(4):
                for t in (2 * g, 2 * g + 1):
                    pe.wait_ge(sem("p_diag"), h * 8 + (t + 1))
                    for k0, k1 in ((0, 4), (4, 8), (8, 10)):
                        for k in range(k0, k1):
                            o = 1536 * (t % 2) + k * P
                            last = mm(PS[:, o:o + P], Pr[t % 2][:, k * P:(k + 1) * P], dgp[:, t % 2, :],
                                      start=True, stop=True)
                        last.then_inc(sem("pt_pe"), 1)
                if g < 3:
                    scores(2 * g + 2)
                    scores(2 * g + 3)
                pe.wait_ge(sem("pt_lo"), h * 24 + (6 * g + 6))
                if g >= 1:
                    pe.wait_ge(sem("o_read"), h * 4 + g)
                o = PS[:, 3072:3072 + 2 * P]
                for k in range(KT):
                    mm(o, Vh[:, k, :], PTh[:, k, :], start=k == 0, stop=False)
                    mm(o, Vh[:, k, :], PTl[:, k, :], start=False, stop=False)
                    last = mm(o, Vl[:, k, :], PTh[:, k, :], start=False, stop=k == KT - 1)
                last.then_inc(sem("pv_done"), 1)
            pe.wait_ge(sem("o_read"), h * 4 + 4)

        J, L = Lin(JOBS["out"]), Lin(SLABS["out"])
        for m in range(9):
            if m < 8:
                gemm(J + m, L + m, XAh, XAl, KD, w8, each_k=sem("br_lo") if m == 0 else None, waited=4,
                     order=(4, 5, 6, 7, 0, 1, 2, 3))
            if m >= 1:
                u = m - 1
                pe.wait_ge(sem("yo_ready"), u + 1)
                if u >= 1:
                    pe.wait_ge(sem("on_ready"), u)
                for t in range(8):
                    last = nc.tensor.transpose(PS[:, ST + t * P:ST + (t + 1) * P], yout[:, u % 2, t * P:(t + 1) * P], ident[:, :])
                last.then_inc(sem("yt_pe"), 1)

    def one(f):
        return f[0], 1

    cqs = at("sq_cq", [P, 2, S], F32, o_xah + 4 * KB4)
    var, sd, rcp = small[:, 0:16], small[:, 16:32], small[:, 32:48]
    ssq, csq = small[:, 48:56], small[:, 56:58]
    Gx, Gc, gfn = small[:, 64:72], small[:, 72:80], small[:, 80:88]
    rql, rqs = small[:, 88:96], small[:, 96:104]
    mx, rsum, nbias = small[:, 104:106], small[:, 106:108], small[:, 108:110]
    tmp8, tmp8b = small[:, 110:118], small[:, 118:126]

    def scalar_program(act):
        fn = nc.scalar.activation

        def root(n, count):
            act.wait_ge(sem("var"), count)
            fn(sd[:, 0:n], var[:, 0:n], ACT.Sqrt).then_inc(sem("sd"), 1)

        act.dma_start(ident[:, :], A["ident"]).then_inc(sem("ident_in"), 16)
        act.dma_start(rotm[:, :], A["rotate"]).then_inc(sem("rotm_in"), 16)
        act.wait_ge(sem("rows_zero"), 1)
        for b, bin_ in enumerate(ROWS):
            r = 0
            for name, n in bin_:
                src = A[name]
                if name in ("q_norm_g_2", "k_norm_g_2"):
                    act.dma_start(rows[r:r + 1, b, :], src[0:1, 0:P]).then_inc(sem("rows_in"), 16)
                    act.dma_start(rows[r + 1:r + 2, b, 0:ROPE], src[0:1, P:QH]).then_inc(sem("rows_in"), 16)
                else:
                    if len(src.shape) == 3:
                        flat = src.rearrange("a k (n p) -> (a k n) p", p=P)
                    elif len(src.shape) == 2:
                        flat = src.rearrange("a (n p) -> (a n) p", p=P)
                    else:
                        flat = src.rearrange("(n p) -> n p", p=P)
                    act.dma_start(rows[r:r + n, b, :], flat).then_inc(sem("rows_in"), 16)
                r += n
        for t in range(9):
            if t < 8:
                act.wait_ge(sem(f"x_in{t % 2}"), 16 * (t // 2 + 1))
                fn(sqj[:, :], xn[:, t % 2, :], ACT.Square, accum_out=ssq[:, t:t + 1]).then_inc(sem("n1_sq"), 1)
                act.wait_ge(sem("row_var"), t + 1)
                fn(sd[:, t:t + 1], var[:, t:t + 1], ACT.Sqrt).then_inc(sem("row_sd"), 1)
            if t >= 1:
                J = Lin(JOBS["x"] + t - 1)
                act.wait_ge(job_done, J.val(1))
                fn(XAh[:, :, (t - 1) * P:t * P], pair(J).rearrange("p (m n) -> p m n", n=P), ACT.Copy).then_inc(sem("x_hi"), 1)
        act.wait_ge(sem("tab_ready"), 1)
        with act.Fori(0, KC) as i:
            J = Lin(JOBS["glu"], 2, i)
            act.wait_ge(job_done, J.val(2))
            act.wait_ge(pair_free[J.slot], J.half())
            fn(T[0][:, 0:S], pair(J + 1), ACT.Sigmoid).then_inc(*one(free(J + 1)))
        with act.Fori(0, 2) as q:
            for u in range(2):
                J = Lin(JOBS["short"] + 3 * u, 6, q)
                act.wait_ge(job_done, J.val(1))
                act.wait_ge(sem("cv_ready"), q * 2 + (u + 1))
                fn(T[0][:, 0:S], pair(J), ACT.Copy).then_inc(*one(free(J)))
                act.wait_ge(sem("s_ready"), q * 2 + (u + 1))
                fn(tile(XBh, q * 2 + (4 + u)), T[3][:, 0:S], ACT.Copy).then_inc(sem("branch_hi"), 1)

        def gate_sigmoid(name, a, b, c0):
            with act.Fori(a, b) as m:
                J = Lin(JOBS[name], 2, m)
                act.wait_ge(job_done, J.val(1))
                act.wait_ge(pair_free[1], (J + 1).half())
                fn(T[0][:, 0:S], pair(J), ACT.Sigmoid, bias=dcol("b_gate", m + c0)).then_inc(*one(free(J)))

        gate_sigmoid("mix_b", 0, 2, 8)
        for i in range(4):
            act.wait_ge(sem("ln_v"), 4 + i)
            if i >= 2:
                act.wait_ge(sem("ln_v"), 8)
            fn(T[2 + i % 2][:, 0:S], conv[:, i, :], ACT.Square).then_inc(sem("ln_sq"), 1)
        gate_sigmoid("mix_b", 2, 4, 8)
        root(8, 1)
        gate_sigmoid("mix_b", 4, 6, 8)
        act.wait_ge(sem("bc_pe"), 1)
        fn(rbc[:, :], PS[:, ST:ST + S], ACT.Copy).then_inc(sem("rbc_ready"), 1)
        for i in range(4):
            act.wait_ge(sem("ln_n"), i + 1)
            if i >= 1:
                act.wait_ge(sem("branch_lo"), 4 + i)
            fn(T[3][:, 0:S], T[1 + i % 2][:, 0:S], ACT.Silu, scale=col("ln_a_g", i), bias=col("ln_a_b", i)).then_inc(sem("a_silu"), 1)
            act.wait_ge(sem("a_silu"), i + 1)
            fn(XBh[:, i, :], T[3][:, 0:S], ACT.Copy).then_inc(sem("branch_hi"), 1)
        gate_sigmoid("mix_b", 6, 8, 8)
        gate_sigmoid("mix_a", 0, 8, 0)
        for m in range(8):
            act.wait_ge(sem("mix_done"), m + 1)
            if m == 0:
                act.wait_ge(job_done, JOBS["wo"])
            fn(XAh[:, m, :], R[:, m, :], ACT.Copy).then_inc(sem("mx_hi"), 1)

        with act.Fori(0, KD // 2) as q:
            for u in range(2):
                J = Lin(JOBS["wo"] + u, 2, q)
                m = q * 2 + u
                act.wait_ge(sem("xt_pe"), q * 2 + (u + 1))
                act.wait_ge(sem("x2_ready"), q * 2 + (u + 1))
                fn(T[0][:, 0:S], PS[:, ST:ST + S], ACT.Copy).then_inc(sem("xt_sb"), 1)
                act.wait_ge(pair_free[u], (J + 0).half() + 1)
                fn(tile(XBh, m), tile(R, m), ACT.Copy, scale=dcol("g_ffn", m)).then_inc(sem("fx_hi"), 1)
                settle(act)
                act.wait_ge(sem("ss_done"), q * 2 + (u + 1))
                fn(T[3][:, 0:S], tile(R, m), ACT.Square).then_inc(sem("fx_sq"), 1)
        act.wait_ge(sem("x2_ready"), 9)
        for t in range(2):
            act.wait_ge(sem("ctx_p_in"), 32)
            if t == 1:
                act.wait_ge(sem("c_sq"), 1)
            fn(T[0][:, 0:S], cstage[:, t, :], ACT.Square, accum_out=csq[:, t:t + 1]).then_inc(sem("c_sq"), 1)
        act.wait_ge(sem("row_var"), 9)
        fn(sd[:, 0:2], var[:, 0:2], ACT.Sqrt).then_inc(sem("row_sd"), 1)
        for t in range(2):
            J = Lin(JOBS["ctx"] + t)
            act.wait_ge(job_done, J.val(1))
            fn(ctxT[:, :, t * P:(t + 1) * P], pair(J).rearrange("p (m n) -> p m n", n=P), ACT.Copy).then_inc(*one(free(J)))
        for k in range(2):
            J = Lin(JOBS["p"] + k)
            act.wait_ge(job_done, J.val(1))
            fn(XAh[:, 4 + k, :], pair(J), ACT.Copy).then_inc(sem("pt_hi"), 1)
        fn(tmp8, tab[:, COL["c_2"]:COL["c_2"] + 8], ACT.Silu).then_inc(sem("cs"), 1)
        fn(tmp8b, tab[:, COL["c_ctx_2"]:COL["c_ctx_2"] + 8], ACT.Silu).then_inc(sem("cs"), 1)
        act.wait_ge(sem("cs"), 2)
        fn(cs_hi[:, :, 0], tmp8, ACT.Copy).then_inc(sem("cs_hi"), 1)
        fn(cs_hi[:, :, 1], tmp8b, ACT.Copy).then_inc(sem("cs_hi"), 1)
        root(8, 2)
        act.wait_ge(sem("bc_pe"), 2)
        act.wait_ge(sem("cols_pe"), 2)
        fn(rbc[:, :], PS[:, ST:ST + S], ACT.Copy).then_inc(sem("rbc_ready"), 1)

        def ffn_chunk(n, slot):
            for k in range(2):
                act.wait_ge(sem("fc_tap"), n * 3 + (3 * k + 3))
                fn(T[2][:, 0:S], T[1][:, 0:S], ACT.Gelu_apprx_tanh).then_inc(sem("gelu"), 1)
                act.wait_ge(sem("f_ready"), n + (k + 1))
                fn(XAh[:, 2 * slot + k, :], T[3][:, 0:S], ACT.Copy).then_inc(sem("f_hi"), 1)

        ffn_chunk(0, 0)
        with act.Fori(0, (NCH - 1) // 2) as q:
            for u in range(2):
                ffn_chunk(q * 4 + (2 * u + 2), 1 - u)
        with act.Fori(0, KD // 2) as q:
            for u in range(2):
                m = q * 2 + u
                act.wait_ge(pair_free[u], (Lin(JOBS["ffn_end"] + u, 2, q)).half() + 1)
                fn(tile(XBh, m), tile(R, m), ACT.Copy, scale=dcol("g_ple", m)).then_inc(sem("gx_hi"), 1)
                act.wait_ge(sem("ss_done"), q * 2 + (u + 9))
                fn(small[:, 126 + u:127 + u], ones[:, 0:1], ACT.Copy)
                fn(T[3][:, 0:S], tile(R, m), ACT.Square).then_inc(sem("gx_sq"), 1)
        root(8, 3)
        act.wait_ge(sem("bc_pe"), 3)
        fn(rbc[:, :], PS[:, ST:ST + S], ACT.Copy).then_inc(sem("rbc_ready"), 1)
        with act.Fori(0, KD) as m:
            act.wait_ge(*free(Lin(JOBS["ple"] + 1, 2, m)))
            fn(T[1][:, 0:S], T[0][:, 0:S], ACT.Sigmoid).then_inc(sem("pg_sig"), 1)
            settle(act)
            act.wait_ge(sem("x4_ready"), m + 1)
            act.wait_ge(sem("s12_done"), m * 2 + 2)
            fn(Q1[:, :], tile(R, m), ACT.Square).then_inc(sem("q12"), 1)
            fn(Q2[:, :], tile(R, m), ACT.Square, scale=dcol("g_final", m)).then_inc(sem("q12"), 1)
        root(8, 4)
        root(8, 5)
        act.wait_ge(sem("bc_pe"), 4)
        fn(rbc[:, :], PS[:, ST:ST + S], ACT.Copy).then_inc(sem("rh_bc"), 1)
        act.wait_ge(sem("bc_pe"), 5)
        fn(T[3][:, 0:S], PS[:, ST:ST + S], ACT.Copy).then_inc(sem("rf_bc"), 1)
        for m in range(8):
            act.wait_ge(sem("h_n"), m + 1)
            if m >= 1:
                act.wait_ge(sem("h_lo"), m)
            fn(T[2][:, 0:S], T[m % 2][:, 0:S], ACT.Identity, scale=Gx[:, m:m + 1], bias=mod_sb[:, m, 0:1]).then_inc(sem("h_f"), 1)
            act.wait_ge(sem("h_f"), m + 1)
            fn(XBh[:, m, :], T[2][:, 0:S], ACT.Copy).then_inc(sem("h_hi"), 1)
        for m in range(8):
            fn(ctxT[:, m, :], ctxT[:, m, :], ACT.Identity, scale=Gc[:, m:m + 1], bias=mod_sb[:, m, 1:2]).then_inc(sem("hc_f"), 1)
        act.wait_ge(sem("hc_f"), 8)
        fn(hch[:, :, :], ctxT[:, :, :], ACT.Copy).then_inc(sem("h_hi"), 1)
        for i in range(4):
            J = Lin(JOBS["ga"] + i)
            act.wait_ge(job_done, J.val(1))
            fn(ga[:, i, :], pair(J), ACT.Silu).then_inc(*one(free(J)))
        J = Lin(JOBS["mla_in"])
        for k, (j, a, b) in enumerate(((J, 0, S), (J + 1, S, NKEY))):
            act.wait_ge(job_done, j.val(1))
            if k == 0:
                act.wait_ge(sem("y_ready"), 8)
            fn(sqck[:, a:b], pair(j, 0, b - a), ACT.Square).then_inc(sem("ck_sq"), 1)
            fn(ckvT[:, a:b], pair(j, 0, b - a), ACT.Copy).then_inc(*one(free(j)))
        for k, (j, a, b) in enumerate(((J + 2, 0, S), (J + 3, S, NKEY))):
            act.wait_ge(job_done, j.val(1))
            fn(sqkr[:, a:b], pair(j, 0, b - a, ROPE), ACT.Square).then_inc(sem("kr_sq"), 1)
            fn(krT[:, a:b], pair(j, 0, b - a, ROPE), ACT.Copy, scale=col("k_norm_g_2", 1, ROPE)).then_inc(sem("kr_sb"), 1)
        for k in range(2):
            j = J + (4 + k)
            act.wait_ge(job_done, j.val(1))
            fn(cqs[:, k, :], pair(j), ACT.Square).then_inc(sem("cq_sq"), 1)
            if k == 0:
                act.wait_ge(sem("y_out"), 8 * 16)
            fn(CQh[:, k, :], pair(j), ACT.Copy, scale=col("q_lora_g_2", k)).then_inc(sem("cq_hi"), 1)
        root(KT, 6)
        act.wait_ge(sem("ck_f"), 1)
        fn(CKh[:, :], ckvT[:, :], ACT.Copy).then_inc(sem("ck_hi"), 1)
        for gq in range(4):
            J = Lin(JOBS["pin"] + gq)
            if gq == 0:
                act.wait_ge(sem("krot_done"), 3)
                act.wait_ge(sem("pads2_zero"), 3)
            else:
                act.wait_ge(sem("pool_ready"), gq)
            act.dma_start(inv[:, :], A["inv_cnt"][gq:gq + 1, :].to_broadcast([P, S])).then_inc(sem("inv_in"), 16)
            act.wait_ge(job_done, J.val(1))
            fn(upad[:, 8:8 + S], pair(J), ACT.Copy).then_inc(*one(free(J)))
            act.wait_ge(sem("pool_ready"), gq + 1)
            if gq == 0:
                act.wait_ge(sem("cols_pe"), 7)
            fn(XAh[:, 4 + gq, :], pl[:, :], ACT.Copy).then_inc(sem("pool_hi"), 1)
            if gq == 0:
                root(8, 7)
        for gq in range(4):
            J = Lin(JOBS["pool"] + 2 * gq)
            act.wait_ge(job_done, J.val(2))
            if gq >= 1:
                act.wait_ge(sem("pool_ready"), 4 + gq)
            fn(sgp[:, :], pair(J + 1), ACT.Silu).then_inc(*one(free(J + 1)))
            act.wait_ge(sem("pool_ready"), 4 + gq + 1)
            fn(XAh[:, 4 + gq, :], pl[:, :], ACT.Copy).then_inc(sem("pool_hi"), 1)
        act.wait_ge(sem("pool_lo"), 8)
        with act.Fori(0, HEADS) as h:
            J = Lin(JOBS["heads"], 6, h)
            act.wait_ge(job_done, J.val(1))
            fn(QNh[:, :], pair(J), ACT.Copy, scale=col("q_norm_g_2", 0)).then_inc(sem("qn_hi"), 1)
            fn(Pr[1][:, 0:S], pair(J), ACT.Square).then_inc(sem("qn_sq"), 1)
            act.wait_ge(job_done, J.val(2))
            fn(U3[0:ROPE, 0:S], pair(J + 1, p=ROPE), ACT.Copy, scale=col("q_norm_g_2", 1, ROPE)).then_inc(sem("qr_sb"), 1)
            fn(dgq[:, :], pair(J + 1, p=ROPE), ACT.Square).then_inc(*one(free(J + 1)))
            act.wait_ge(job_done, J.val(4))
            fn(Pr[0][:, 0:S], pair(J + 2), ACT.Square).then_inc(sem("kn_sq"), 1)
            fn(Pr[0][:, S:NKEY], pair(J + 3, 0, CTX), ACT.Square).then_inc(sem("kn_sq"), 1)
            act.wait_ge(sem("head_var"), h * 2 + 1)
            fn(sd[:, 0:KT], var[:, 0:KT], ACT.Sqrt).then_inc(sem("head_sd"), 1)
            act.wait_ge(sem("qr_f"), h + 1)
            fn(QRh[:, :], U3[0:ROPE, 0:S], ACT.Copy).then_inc(sem("qr_hi"), 1)
            act.wait_ge(sem("kbc"), h + 1)
            fn(rb_h[:, :], PS[:, ST:ST + NKEY], ACT.Copy).then_inc(sem("rb_h"), 1)
            act.wait_ge(sem("kn_f"), h * 2 + 2)
            fn(KNh[:, :], Pr[0][:, :], ACT.Copy).then_inc(sem("kn_hi"), 1)
            for k, (a, b) in enumerate(((0, 8), (8, KT))):
                act.wait_ge(job_done, J.val(5 + k))
                fn(Vh[:, a:b, :], pair(J + (4 + k), 0, (b - a) * P).rearrange("p (t n) -> p t n", n=P), ACT.Copy).then_inc(sem("v_hi"), 1)
            act.wait_ge(sem("kr_f"), h + 1)
            fn(KRh[:, :], U3[0:ROPE, :], ACT.Copy).then_inc(sem("kr_hi"), 1)
            act.wait_ge(sem("head_var"), h * 2 + 2)
            fn(sd[:, 0:8], var[:, 0:8], ACT.Sqrt).then_inc(sem("head_sd"), 1)

            def exponentials(t):
                act.wait_ge(sem("nbias"), h * 8 + (t + 1))
                fn(Pr[t % 2][:, :], PS[:, 1536 * (t % 2):1536 * (t % 2) + NKEY], ACT.Exp,
                   scale=rqs[:, t:t + 1], bias=nbias[:, t % 2:t % 2 + 1],
                   accum_out=rsum[:, t % 2:t % 2 + 1]).then_inc(sem("p_exp"), 1)

            exponentials(0)
            exponentials(1)
            for g in range(4):
                if g >= 1:
                    act.wait_ge(sem("pv_done"), h * 4 + g)
                for t in (2 * g, 2 * g + 1):
                    for n, (k0, k1) in enumerate(((0, 4), (4, 8), (8, 10))):
                        o = 1536 * (t % 2)
                        act.wait_ge(sem("pt_pe"), h * 24 + (3 * t + n + 1))
                        fn(PTh[:, k0:k1, P * (t % 2):P * (t % 2 + 1)],
                           PS[:, o + k0 * P:o + k1 * P].rearrange("p (t n) -> p t n", n=P),
                           ACT.Copy).then_inc(sem("pt_hi_"), 1)
                if g < 3:
                    exponentials(2 * g + 2)
                    exponentials(2 * g + 3)
        act.wait_ge(sem("o_read"), 4 * HEADS)
        for h in range(HEADS):
            fn(XAh[:, h, :], ga[:, h, :], ACT.Copy).then_inc(sem("br_hi"), 1)
        for m in range(8):
            act.wait_ge(sem("yt_pe"), m + 1)
            if m >= 2:
                act.wait_ge(sem(f"out_done{m % 2}"), 16 * (m // 2))
            fn(onat[:, m % 2, :, :].rearrange("p t n -> p (t n)"), PS[:, ST:ST + S], ACT.Copy).then_inc(sem("on_ready"), 1)

    def vector_program(dve):
        tt, ts, stt = nc.vector.tensor_tensor, nc.vector.tensor_scalar, nc.vector.scalar_tensor_tensor

        marks = [0]

        def after_all(s, k):
            marks[0] += 1
            c = 58 + marks[0] % 6
            nc.vector.memset(small[:, c:c + 1], 0.0).then_inc(s, k)

        def rstd(n, width, cols, count, roots, dg=None, dcount=None, at_col=0, to=None):
            dve.wait_ge(sem("cols_pe"), cols)
            ts(var[:, 0:n], PS[:, SC + at_col:SC + at_col + n], 1.0 / width, EPS, ALU.mult, ALU.add).then_inc(sem("var"), 1)
            dve.wait_ge(sem("sd"), count)
            to = rcp[:, 0:n] if to is None else to
            nc.vector.reciprocal(to, sd[:, 0:n]).then_inc(sem("rcp"), 1)
            dve.wait_ge(sem("rcp"), roots)
            if dg is not None:
                diagonals(dg, n, to)

        def diagonals(dg, n, src):
            tt(dg, ident[:, :].unsqueeze(1).to_broadcast([P, n, P]), src.unsqueeze(2).to_broadcast([P, n, P]),
               ALU.mult).then_inc(sem("diag"), 1)

        nc.vector.memset(rows[:, :, :], 0.0).then_inc(sem("rows_zero"), 1)
        nc.vector.memset(ones[:, :], 1.0).then_inc(sem("ones_set"), 1)
        dve.wait_ge(sem("g_in"), 16)
        for t in range(9):
            if t < 8:
                dve.wait_ge(sem("n1_sq"), t + 1)
                ts(var[:, t:t + 1], ssq[:, t:t + 1], 1.0 / D, EPS, ALU.mult, ALU.add).then_inc(sem("row_var"), 1)
                dve.wait_ge(sem("row_sd"), t + 1)
                nc.vector.reciprocal(rcp[:, t:t + 1], sd[:, t:t + 1]).then_inc(sem("row_rcp"), 1)
                dve.wait_ge(sem("row_rcp"), t + 1)
                if t >= 2:
                    dve.wait_ge(job_done, t - 1)
                stt(xs[:, t % 2, :], xn[:, t % 2, :], rcp[:, t:t + 1], gbc[:, :], ALU.mult, ALU.mult).then_inc(sem("xs_ready"), 1)
            if t >= 1:
                J = Lin(JOBS["x"] + t - 1)
                dve.wait_ge(sem("x_hi"), t)
                tt(XAl[:, :, (t - 1) * P:t * P], pair(J).rearrange("p (m n) -> p m n", n=P),
                   f32(XAh[:, :, (t - 1) * P:t * P]), ALU.subtract).then_inc(*one(free(J)))
        dve.wait_ge(sem("tab_pe"), 1)
        nc.vector.tensor_copy(tab[:, :], PS[:, ST:ST + 3 * P]).then_inc(sem("tab_ready"), 1)
        nc.vector.memset(gpad[:, :, 0:LPAD], 0.0).then_inc(sem("pads_zero"), 1)
        nc.vector.memset(T[1][:, 0:2], 0.0).then_inc(sem("pads_zero"), 1)
        nc.vector.memset(rbc[:, 0:8], 0.0).then_inc(sem("cv_ready"), 1)
        dve.wait_ge(sem("pads_zero"), 2)
        dve.wait_ge(sem("tab_ready"), 1)

        def tap(i, k, count):
            src = tile(gpad, i, k, k + S)
            if k == 0:
                ts(tile(conv, i), src, dcol("conv_a_w", i), dcol("conv_a_b", i), ALU.mult, ALU.add).then_inc(sem("conv_tap"), 1)
            else:
                dve.wait_ge(sem("conv_tap"), count)
                stt(tile(conv, i), src, dcol("conv_a_w", i + 4 * k), tile(conv, i), ALU.mult, ALU.add).then_inc(sem("conv_tap"), 1)

        N1 = 14
        with dve.Fori(0, KC) as i:
            J = Lin(JOBS["glu"], 2, i)
            dve.wait_ge(*free(J + 1))
            tt(tile(gpad, i, LPAD, LPAD + S), pair(J), T[0][:, 0:S], ALU.mult).then_inc(*one(free(J)))
            dve.wait_ge(*free(J))
            for k in range(N1):
                tap(i, k, i * N1 + k)
        N2 = TAPS_A - N1
        with dve.Fori(0, 2) as q:
            for u in range(2):
                i = q * 2 + u
                J = Lin(JOBS["short"] + 3 * u, 6, q)
                dve.wait_ge(job_done, J.val(2))
                dve.wait_ge(*free(J))
                tt(T[1][:, 2:2 + S], pair(J + 1), T[0][:, 0:S], ALU.mult).then_inc(*one(free(J + 1)))
                dve.wait_ge(*free(J + 1))
                ts(T[2][:, 0:S], T[1][:, 0:S], dcol("conv_b_w", i), None, ALU.mult).then_inc(sem("cv_ready"), 1)
                for k in range(1, TAPS_B):
                    if k == 1:
                        dve.wait_ge(sem("cv_ready"), q * 2 + (u + 2))
                    else:
                        dve.wait_ge(sem("short_tap"), q * 4 + (2 * u + k - 1))
                    stt(T[2][:, 0:S], T[1][:, k:k + S], dcol("conv_b_w", i + 4 * k), T[2][:, 0:S],
                        ALU.mult, ALU.add).then_inc(sem("short_tap"), 1)
                for k in range(N1, N1 + N2 // 2):
                    tap(i, k, i * N2 + (KC * N1 + k - N1))
                dve.wait_ge(job_done, J.val(3))
                dve.wait_ge(sem("short_tap"), q * 4 + (2 * u + 2))
                tt(T[3][:, 0:S], pair(J + 2), T[2][:, 0:S], ALU.mult).then_inc(sem("s_ready"), 1)
                nc.vector.memset(T[1][:, 0:2], 0.0).then_inc(*one(free(J + 2)))
                for k in range(N1 + N2 // 2, TAPS_A):
                    tap(i, k, i * N2 + (KC * N1 + k - N1))
                dve.wait_ge(sem("branch_hi"), q * 2 + (u + 1))
                tt(tile(XBl, q * 2 + (4 + u)), T[3][:, 0:S], f32(tile(XBh, q * 2 + (4 + u))),
                   ALU.subtract).then_inc(sem("branch_lo"), 1)

        def mix(name, a, b, add):
            with dve.Fori(a, b) as m:
                J = Lin(JOBS[name], 2, m)
                dve.wait_ge(job_done, J.val(2))
                dve.wait_ge(*free(J))
                if not add:
                    tt(tile(R, m), pair(J + 1), T[0][:, 0:S], ALU.mult).then_inc(*one(free(J + 1)))
                else:
                    tt(T[1][:, 0:S], pair(J + 1), T[0][:, 0:S], ALU.mult).then_inc(*one(free(J + 1)))
                    dve.wait_ge(*free(J + 1))
                    tt(tile(R, m), tile(R, m), T[1][:, 0:S], ALU.add).then_inc(sem("mix_done"), 1)
                    dve.wait_ge(sem("mix_done"), m + 1)

        v = [0]

        def ln_step(ins):
            v[0] += 1
            ins.then_inc(sem("ln_v"), 1)

        dve.wait_ge(sem("conv_tap"), KC * TAPS_A)
        ln_step(tt(T[1][:, 0:S], conv[:, 0, :], conv[:, 1, :], ALU.add))
        for i in (2, 3):
            dve.wait_ge(sem("ln_v"), v[0])
            ln_step(tt(T[1][:, 0:S], T[1][:, 0:S], conv[:, i, :], ALU.add))
        mix("mix_b", 0, 2, False)
        dve.wait_ge(sem("ln_pe"), 1)
        for i in range(4):
            ln_step(stt(conv[:, i, :], PS[:, ST:ST + S], -1.0 / DC, conv[:, i, :], ALU.mult, ALU.add))
        dve.wait_ge(sem("ln_sq"), 2)
        ln_step(tt(T[1][:, 0:S], T[2][:, 0:S], T[3][:, 0:S], ALU.add))
        for i in (2, 3):
            dve.wait_ge(sem("ln_sq"), 1 + i)
            dve.wait_ge(sem("ln_v"), v[0])
            ln_step(tt(T[1][:, 0:S], T[1][:, 0:S], T[i][:, 0:S], ALU.add))
        mix("mix_b", 2, 4, False)
        rstd(8, DC, 1, 1, 1, T[2][:, 0:1024].rearrange("p (t n) -> p t n", n=P))
        mix("mix_b", 4, 6, False)
        dve.wait_ge(sem("rbc_ready"), 1)
        for i in range(5):
            if i < 4:
                if i >= 2:
                    dve.wait_ge(sem("a_silu"), i - 1)
                tt(T[1 + i % 2][:, 0:S], conv[:, i, :], rbc[:, :], ALU.mult).then_inc(sem("ln_n"), 1)
            if i >= 1:
                dve.wait_ge(sem("branch_hi"), 4 + i)
                dve.wait_ge(sem("ln_n"), i)
                tt(XBl[:, i - 1, :], T[3][:, 0:S], f32(XBh[:, i - 1, :]), ALU.subtract).then_inc(sem("branch_lo"), 1)
        mix("mix_b", 6, 8, False)
        mix("mix_a", 0, 8, True)
        for m in range(8):
            dve.wait_ge(sem("mx_hi"), m + 1)
            tt(XAl[:, m, :], R[:, m, :], f32(XAh[:, m, :]), ALU.subtract).then_inc(sem("mx_lo"), 1)
        nc.vector.memset(rbc[:, :], 0.0).then_inc(sem("ss_done0"), 1)
        dve.wait_ge(sem("ss_done0"), 1)
        after_all(sem("x2_ready"), 1)
        after_all(sem("ss_done"), 1)

        def residual_tail(m, hi, lo, sq, gname, mval, sbase):
            dve.wait_ge(sem(hi), mval)
            stt(tile(XBl, m), tile(R, m), dcol(gname, m), f32(tile(XBh, m)), ALU.mult, ALU.subtract).then_inc(sem(lo), 1)
            dve.wait_ge(sem(sq), mval)
            tt(rbc[:, :], rbc[:, :], T[3][:, 0:S], ALU.add).then_inc(sem("ss_done"), 1)

        with dve.Fori(0, KD // 2) as q:
            for u in range(2):
                m = q * 2 + u
                J = Lin(JOBS["wo"] + u, 2, q)
                dve.wait_ge(job_done, J.val(1))
                dve.wait_ge(sem("xt_sb"), q * 2 + (u + 1))
                tt(tile(R, m), pair(J), T[0][:, 0:S], ALU.add).then_inc(*one(free(J)))
                dve.wait_ge(*free(J))
                after_all(sem("x2_ready"), 1)
                residual_tail(m, "fx_hi", "fx_lo", "fx_sq", "g_ffn", q * 2 + (u + 1), 0)
                dve.wait_ge(sem("ss_done"), q * 2 + (u + 2))
        dve.wait_ge(sem("c_sq"), 2)
        ts(var[:, 0:2], csq[:, 0:2], 1.0 / D, EPS, ALU.mult, ALU.add).then_inc(sem("row_var"), 1)
        dve.wait_ge(sem("row_sd"), 9)
        nc.vector.reciprocal(rcp[:, 0:2], sd[:, 0:2]).then_inc(sem("row_rcp"), 1)
        dve.wait_ge(sem("row_rcp"), 9)
        for t in range(2):
            ts(cstage[:, t, :], cstage[:, t, :], rcp[:, t:t + 1], None, ALU.mult).then_inc(sem("cs_ready"), 1)
        for k in range(2):
            J = Lin(JOBS["p"] + k)
            dve.wait_ge(sem("pt_hi"), k + 1)
            tt(XAl[:, 4 + k, :], pair(J), f32(XAh[:, 4 + k, :]), ALU.subtract).then_inc(*one(free(J)))
        dve.wait_ge(sem("cs_hi"), 2)
        tt(cs_lo[:, :, 0], tmp8, f32(cs_hi[:, :, 0]), ALU.subtract)
        tt(cs_lo[:, :, 1], tmp8b, f32(cs_hi[:, :, 1]), ALU.subtract).then_inc(sem("cs_lo"), 1)
        nc.vector.memset(T[0][:, 0:2], 0.0).then_inc(sem("pads_zero"), 1)
        rstd(8, D, 2, 2, 2, T[3][:, 0:1024].rearrange("p (t n) -> p t n", n=P))
        dve.wait_ge(sem("pads_zero"), 3)
        dve.wait_ge(sem("rbc_ready"), 2)

        def ffn_chunk(J, n, slot):
            for k in range(2):
                Jg = J + 2 * k
                dve.wait_ge(job_done, Jg.val(1))
                tt(T[0][:, 2:2 + S], pair(Jg), rbc[:, :], ALU.mult).then_inc(*one(free(Jg)))
                dve.wait_ge(*free(Jg))
                ts(T[1][:, 0:S], T[0][:, 0:S], dcol("conv_f_w", n + k), dcol("conv_f_b", n + k), ALU.mult, ALU.add).then_inc(sem("fc_tap"), 1)
                for w in range(1, TAPS_F):
                    dve.wait_ge(sem("fc_tap"), n * 3 + (3 * k + w))
                    stt(T[1][:, 0:S], T[0][:, w:w + S], dcol("conv_f_w", n + (k + NF * w)), T[1][:, 0:S],
                        ALU.mult, ALU.add).then_inc(sem("fc_tap"), 1)
                dve.wait_ge(job_done, Jg.val(2))
                tt(T[3][:, 0:S], pair(Jg + 1), rbc[:, :], ALU.mult).then_inc(*one(free(Jg + 1)))
                dve.wait_ge(*free(Jg + 1))
                dve.wait_ge(sem("gelu"), n + (k + 1))
                tt(T[3][:, 0:S], T[3][:, 0:S], T[2][:, 0:S], ALU.mult).then_inc(sem("f_ready"), 1)
                dve.wait_ge(sem("f_hi"), n + (k + 1))
                tt(XAl[:, 2 * slot + k, :], T[3][:, 0:S], f32(XAh[:, 2 * slot + k, :]), ALU.subtract).then_inc(sem("f_lo"), 1)

        def read_mod(n, count):
            dve.wait_ge(sem("mod_pe"), count)
            for k in range(2):
                last = ts(tile(mod_sb, n + k, 0, 2), PS[:, SC + 64 + 2 * k:SC + 66 + 2 * k], dcol("b_mod_2", n + k), None, ALU.add)
            last.then_inc(sem("mod_read"), 1)

        def down(J):
            for m in range(8):
                dve.wait_ge(job_done, J.val(m + 1))
                tt(R[:, m, :], pair(J + m), R[:, m, :], ALU.add).then_inc(*one(free(J + m)))

        ffn_chunk(Lin(JOBS["ffn"]), 0, 0)
        read_mod(0, 2)
        with dve.Fori(0, (NCH - 1) // 2) as q:
            for u in range(2):
                J = Lin(JOBS["ffn_loop"] + 12 * u, 24, q)
                ffn_chunk(J, q * 4 + (2 * u + 2), 1 - u)
                read_mod(q * 4 + (2 * u + 2), q * 4 + (2 * u + 4))
                down(J + 4)
        nc.vector.memset(rbc[:, :], 0.0).then_inc(sem("ss_done0"), 1)
        dve.wait_ge(sem("ss_done0"), 2)
        with dve.Fori(0, KD // 2) as q:
            for u in range(2):
                m = q * 2 + u
                J = Lin(JOBS["ffn_end"] + u, 2, q)
                dve.wait_ge(job_done, J.val(1))
                tt(tile(R, m), pair(J), tile(R, m), ALU.add).then_inc(*one(free(J)))
                dve.wait_ge(*free(J))
                residual_tail(m, "gx_hi", "gx_lo", "gx_sq", "g_ple", q * 2 + (u + 1), 8)
                dve.wait_ge(sem("ss_done"), q * 2 + (u + 10))
        read_mod(2 * NCH, 2 * NCH + 2)
        rstd(8, D, 3, 3, 3, T[3][:, 0:1024].rearrange("p (t n) -> p t n", n=P))
        nc.vector.memset(S1[:, :], 0.0).then_inc(sem("s12_done"), 1)
        nc.vector.memset(S2[:, :], 0.0).then_inc(sem("s12_done"), 1)
        dve.wait_ge(sem("rbc_ready"), 3)
        with dve.Fori(0, KD) as m:
            J = Lin(JOBS["ple"], 2, m)
            dve.wait_ge(job_done, J.val(2))
            tt(T[0][:, 0:S], pair(J + 1), rbc[:, :], ALU.mult).then_inc(*one(free(J + 1)))
            dve.wait_ge(sem("pg_sig"), m + 1)
            tt(T[2][:, 0:S], pair(J), T[1][:, 0:S], ALU.mult).then_inc(*one(free(J)))
            dve.wait_ge(*free(J))
            tt(tile(R, m), tile(R, m), T[2][:, 0:S], ALU.add).then_inc(sem("x4_ready"), 1)
            dve.wait_ge(sem("q12"), m * 2 + 2)
            dve.wait_ge(sem("s12_done"), m * 2 + 2)
            tt(S1[:, :], S1[:, :], Q1[:, :], ALU.add).then_inc(sem("s12_done"), 1)
            tt(S2[:, :], S2[:, :], Q2[:, :], ALU.add).then_inc(sem("s12_done"), 1)
        c = [0]

        def link(ins):
            c[0] += 1
            ins.then_inc(sem("chain"), 1)
            dve.wait_ge(sem("chain"), c[0])

        rf, rh = rql, rqs
        rstd(8, D, 5, 4, 4, to=rf)
        link(tt(tmp8, rf, rf, ALU.mult))
        link(tt(tmp8, PS[:, SC + 8:SC + 16], tmp8, ALU.mult))
        ts(var[:, 0:8], tmp8, 1.0 / D, EPS, ALU.mult, ALU.add).then_inc(sem("var"), 1)
        dve.wait_ge(sem("sd"), 5)
        link(nc.vector.reciprocal(tmp8, sd[:, 0:8]))
        link(tt(rh, rf, tmp8, ALU.mult))
        diagonals(Q1[:, :].rearrange("p (t n) -> p t n", n=P), 8, rh)
        diagonals(Q2[:, :].rearrange("p (t n) -> p t n", n=P), 8, rf)
        dve.wait_ge(sem("mod_read"), NCH + 1)
        gfc = tab[:, COL["g_final"]:COL["g_final"] + 8]
        ngc = tab[:, COL["norm_g_2"]:COL["norm_g_2"] + 8]
        link(ts(tmp8, mod_sb[:, 8:16, 0], 1.0, None, ALU.add))
        link(tt(tmp8, tmp8, ngc, ALU.mult))
        link(tt(Gx, tmp8, gfc, ALU.mult))
        link(ts(tmp8b, mod_sb[:, 8:16, 1], 1.0, None, ALU.add))
        link(tt(Gc, tmp8b, ngc, ALU.mult))
        dve.wait_ge(sem("rh_bc"), 1)
        for m in range(9):
            if m < 8:
                if m >= 2:
                    dve.wait_ge(sem("h_f"), m - 1)
                tt(T[m % 2][:, 0:S], R[:, m, :], rbc[:, :], ALU.mult).then_inc(sem("h_n"), 1)
            if m >= 1:
                dve.wait_ge(sem("h_hi"), m)
                tt(XBl[:, m - 1, :], T[2][:, 0:S], f32(XBh[:, m - 1, :]), ALU.subtract).then_inc(sem("h_lo"), 1)
        dve.wait_ge(sem("h_hi"), 9)
        tt(hcl[:, :, :], ctxT[:, :, :], f32(hch[:, :, :]), ALU.subtract).then_inc(sem("h_lo"), 1)
        dve.wait_ge(sem("rf_bc"), 1)
        for m in range(8):
            stt(R[:, m, :], R[:, m, :], col("g_final", m), T[3][:, 0:S], ALU.mult, ALU.mult).then_inc(sem("y_ready"), 1)
        dve.wait_ge(sem("kr_sb"), 2)
        after_all(*one(free(Lin(JOBS["mla_in"] + 2))))
        after_all(*one(free(Lin(JOBS["mla_in"] + 3))))
        dve.wait_ge(sem("rope_in"), 32)
        dve.wait_ge(sem("y_out"), 8 * 16)
        dve.wait_ge(sem("rot_pe"), 1)
        tt(U3[0:ROPE, 0:S], PS[0:ROPE, ST:ST + S], sinb[:, :], ALU.mult).then_inc(sem("krot_mul"), 1)
        tt(krot[:, 0:S], krT[:, 0:S], cosb[:, :], ALU.mult).then_inc(sem("krot_done"), 1)
        nc.vector.tensor_copy(krot[:, S:NKEY], krT[:, S:NKEY]).then_inc(sem("krot_done"), 1)
        dve.wait_ge(sem("krot_mul"), 1)
        dve.wait_ge(sem("krot_done"), 2)
        tt(krot[:, 0:S], krot[:, 0:S], U3[0:ROPE, 0:S], ALU.add).then_inc(sem("krot_done"), 1)
        for k in range(2):
            J = Lin(JOBS["mla_in"] + 4 + k)
            dve.wait_ge(sem("cq_hi"), k + 1)
            stt(CQl[:, k, :], pair(J), col("q_lora_g_2", k), f32(CQh[:, k, :]), ALU.mult, ALU.subtract).then_inc(sem("cq_lo"), 1)
            after_all(*one(free(J)))
        dve.wait_ge(sem("cq_sq"), 2)
        tt(cqs[:, 0, :], cqs[:, 0, :], cqs[:, 1, :], ALU.add).then_inc(sem("cq_ss"), 1)
        rstd(KT, 128, 6, 6, 5, dgck[:, :, :])
        dve.wait_ge(sem("bc_pe"), 6)
        stt(ckvT[:, :], ckvT[:, :], col("kv_lora_g_2", 0), PS[:, ST:ST + NKEY], ALU.mult, ALU.mult).then_inc(sem("ck_f"), 1)
        dve.wait_ge(sem("ck_hi"), 1)
        tt(CKl[:, :], ckvT[:, :], f32(CKh[:, :]), ALU.subtract).then_inc(sem("ck_lo"), 1)
        for x in (upad, wA, wB):
            nc.vector.memset(x[:, :], 0.0).then_inc(sem("pads2_zero"), 1)
        dve.wait_ge(sem("pads2_zero"), 3)
        n = [0]
        for gq in range(4):
            J = Lin(JOBS["pin"] + gq)
            dve.wait_ge(*free(J))
            src, ln = upad, TB // 4
            for s in range(gq + 1):
                dst = wA if s % 2 == 0 else wB
                sh = 1 << s
                ln -= sh
                if s:
                    dve.wait_ge(sem("win"), n[0])
                tt(dst[:, 0:ln], src[:, 0:ln], src[:, sh:sh + ln], ALU.add).then_inc(sem("win"), 1)
                n[0] += 1
                src = dst
            w = WINDOWS[gq]
            dve.wait_ge(sem("win"), n[0])
            dve.wait_ge(sem("inv_in"), 16 * (gq + 1))
            if gq >= 1:
                dve.wait_ge(sem("pool_lo"), gq)
                dve.wait_ge(sem("pool_hi"), gq)
            else:
                dve.wait_ge(sem("ck_lo"), 1)
            a = 8 - w // 2
            tt(pl[:, :], src[:, a:a + S], inv[:, :], ALU.mult).then_inc(sem("pl_mul"), 1)
            dve.wait_ge(sem("pl_mul"), gq + 1)
            tt(pl[:, :], pl[:, :], upad[:, 8:8 + S], ALU.subtract).then_inc(sem("pool_ready"), 1)
            dve.wait_ge(sem("pool_hi"), gq + 1)
            tt(XAl[:, 4 + gq, :], pl[:, :], f32(XAh[:, 4 + gq, :]), ALU.subtract).then_inc(sem("pool_lo"), 1)
            if gq == 0:
                rstd(8, 256, 7, 7, 6, at_col=16, to=rql)
        for gq in range(4):
            J = Lin(JOBS["pool"] + 2 * gq)
            dve.wait_ge(*free(J + 1))
            if gq == 0:
                dve.wait_ge(sem("pool_lo"), 4)
            else:
                dve.wait_ge(sem("pool_lo"), 4 + gq)
            stt(pl[:, :], pair(J), col("pool_scale_2", gq), sgp[:, :], ALU.mult, ALU.mult).then_inc(sem("pool_ready"), 1)
            after_all(*one(free(J)))
            dve.wait_ge(sem("pool_hi"), 4 + gq + 1)
            tt(XAl[:, 4 + gq, :], pl[:, :], f32(XAh[:, 4 + gq, :]), ALU.subtract).then_inc(sem("pool_lo"), 1)
        dve.wait_ge(sem("rope_in"), 64)
        with dve.Fori(0, HEADS) as h:
            J = Lin(JOBS["heads"], 6, h)
            dve.wait_ge(sem("qn_hi"), h + 1)
            dve.wait_ge(sem("qn_sq"), h + 1)
            stt(QNl[:, :], pair(J), col("q_norm_g_2", 0), f32(QNh[:, :]), ALU.mult, ALU.subtract).then_inc(*one(free(J)))
            dve.wait_ge(*free(J + 1))
            tt(Pr[1][0:ROPE, 0:S], Pr[1][0:ROPE, 0:S], dgq[:, :], ALU.add).then_inc(sem("qsq"), 1)
            dve.wait_ge(sem("kn_sq"), h * 2 + 2)
            tt(Pr[0][0:ROPE, :], Pr[0][0:ROPE, :], sqkr[:, :], ALU.add).then_inc(sem("ksq"), 1)
            dve.wait_ge(sem("qrot_pe"), h + 1)
            dve.wait_ge(sem("qsq"), h + 1)
            tt(dgq[:, :], PS[0:ROPE, ST:ST + S], sinq[:, :], ALU.mult).then_inc(sem("qr_a"), 1)
            tt(U3[0:ROPE, 0:S], U3[0:ROPE, 0:S], cosq[:, :], ALU.mult).then_inc(sem("qr_a"), 1)
            dve.wait_ge(sem("qr_a"), h * 2 + 2)
            tt(U3[0:ROPE, 0:S], U3[0:ROPE, 0:S], dgq[:, :], ALU.add).then_inc(sem("qr_f"), 1)
            dve.wait_ge(sem("kcols"), h + 1)
            ts(var[:, 0:KT], PS[:, SC:SC + KT], 1.0 / QH, EPS, ALU.mult, ALU.add).then_inc(sem("head_var"), 1)
            dve.wait_ge(sem("head_sd"), h * 2 + 1)
            nc.vector.reciprocal(rcp[:, 0:KT], sd[:, 0:KT]).then_inc(sem("krcp"), 1)
            dve.wait_ge(sem("krcp"), h + 1)
            tt(dgh[:, :, :], ident[:, :].unsqueeze(1).to_broadcast([P, KT, P]),
               rcp[:, 0:KT].unsqueeze(2).to_broadcast([P, KT, P]), ALU.mult).then_inc(sem("kdiag"), 1)
            dve.wait_ge(sem("qr_hi"), h + 1)
            tt(QRl[:, :], U3[0:ROPE, 0:S], f32(QRh[:, :]), ALU.subtract).then_inc(sem("qr_lo"), 1)
            dve.wait_ge(sem("rb_h"), h + 1)
            stt(Pr[0][:, 0:S], pair(J + 2), col("k_norm_g_2", 0), rb_h[:, 0:S], ALU.mult, ALU.mult).then_inc(sem("kn_f"), 1)
            stt(Pr[0][:, S:NKEY], pair(J + 3, 0, CTX), col("k_norm_g_2", 0), rb_h[:, S:NKEY], ALU.mult, ALU.mult).then_inc(sem("kn_f"), 1)
            after_all(*one(free(J + 2)))
            after_all(*one(free(J + 3)))
            dve.wait_ge(sem("qr_lo"), h + 1)
            tt(U3[0:ROPE, :], krot[:, :], rb_h[0:ROPE, :], ALU.mult).then_inc(sem("kr_f"), 1)
            dve.wait_ge(sem("kn_hi"), h + 1)
            tt(KNl[:, :], Pr[0][:, :], f32(KNh[:, :]), ALU.subtract).then_inc(sem("kn_lo"), 1)
            for k, (a, b) in enumerate(((0, 8), (8, KT))):
                dve.wait_ge(sem("v_hi"), h * 2 + (k + 1))
                tt(Vl[:, a:b, :], pair(J + (4 + k), 0, (b - a) * P).rearrange("p (t n) -> p t n", n=P), f32(Vh[:, a:b, :]),
                   ALU.subtract).then_inc(sem("v_lo"), 1)
                after_all(*one(free(J + (4 + k))))
            dve.wait_ge(sem("kr_hi"), h + 1)
            tt(KRl[:, :], U3[0:ROPE, :], f32(KRh[:, :]), ALU.subtract).then_inc(sem("kr_lo"), 1)
            dve.wait_ge(sem("qcols"), h + 1)
            tt(tmp8, rql, rql, ALU.mult).then_inc(sem("qf"), 1)
            dve.wait_ge(sem("qf"), h * 4 + 1)
            tt(tmp8, PS[:, SC + 16:SC + 24], tmp8, ALU.mult).then_inc(sem("qf"), 1)
            dve.wait_ge(sem("qf"), h * 4 + 2)
            ts(var[:, 0:8], tmp8, 1.0 / QH, EPS, ALU.mult, ALU.add).then_inc(sem("head_var"), 1)
            dve.wait_ge(sem("head_sd"), h * 2 + 2)
            nc.vector.reciprocal(tmp8, sd[:, 0:8]).then_inc(sem("qf"), 1)
            dve.wait_ge(sem("qf"), h * 4 + 3)
            stt(rqs, tmp8, SCALE, rql, ALU.mult, ALU.mult).then_inc(sem("qf"), 1)
            dve.wait_ge(sem("qf"), h * 4 + 4)

            def maxima(t):
                a = t % 2
                dve.wait_ge(sem("s_done"), h * 8 + (t + 1))
                nc.vector.reduce_max(mx[:, a:a + 1], PS[:, 1536 * a:1536 * a + NKEY], AX.X).then_inc(sem("mx"), 1)
                dve.wait_ge(sem("mx"), h * 8 + (t + 1))
                stt(nbias[:, a:a + 1], mx[:, a:a + 1], -1.0, rqs[:, t:t + 1], ALU.mult, ALU.mult).then_inc(sem("nbias"), 1)

            def diagonal(t):
                a = t % 2
                dve.wait_ge(sem("p_exp"), h * 8 + (t + 1))
                nc.vector.reciprocal(rsum[:, a:a + 1], rsum[:, a:a + 1]).then_inc(sem("rs"), 1)
                dve.wait_ge(sem("rs"), h * 8 + (t + 1))
                ts(dgp[:, a, :], ident[:, :], rsum[:, a:a + 1], None, ALU.mult).then_inc(sem("p_diag"), 1)

            for t in range(2):
                maxima(t)
                diagonal(t)
            for g in range(4):
                for t in (2 * g, 2 * g + 1):
                    for n, (k0, k1) in enumerate(((0, 4), (4, 8), (8, 10))):
                        o = 1536 * (t % 2)
                        dve.wait_ge(sem("pt_hi_"), h * 24 + (3 * t + n + 1))
                        cols = slice(P * (t % 2), P * (t % 2 + 1))
                        tt(PTl[:, k0:k1, cols], PS[:, o + k0 * P:o + k1 * P].rearrange("p (t n) -> p t n", n=P),
                           f32(PTh[:, k0:k1, cols]), ALU.subtract).then_inc(sem("pt_lo"), 1)
                if g < 3:
                    for t in (2 * g + 2, 2 * g + 3):
                        maxima(t)
                        diagonal(t)
                dve.wait_ge(sem("pv_done"), h * 4 + (g + 1))
                part = tile(ga, h).rearrange("p (q t) -> p t q", t=8)[:, 2 * g:2 * g + 2, :]
                tt(part, PS[:, 3072:3072 + 2 * P].rearrange("p (t q) -> p t q", t=2), part, ALU.mult).then_inc(sem("o_read"), 1)
        for h in range(HEADS):
            dve.wait_ge(sem("br_hi"), h + 1)
            tt(XAl[:, h, :], ga[:, h, :], f32(XAh[:, h, :]), ALU.subtract).then_inc(sem("br_lo"), 1)
        for m in range(8):
            J = Lin(JOBS["out"] + m)
            dve.wait_ge(job_done, J.val(1))
            if m == 0:
                dve.wait_ge(sem("y_in"), 8 * 16)
            if m >= 2:
                dve.wait_ge(sem("yt_pe"), m - 1)
            stt(yout[:, m % 2, :], pair(J), mod_sb[:, 16 + m, 0:1], ybuf[:, m, :], ALU.mult, ALU.add).then_inc(sem("yo_ready"), 1)
            after_all(*one(free(J)))

    dgq = at("q_sin", [ROPE, S], F32, o_t)
    with nc.Block() as block:
        @block.sync
        def _(sp):
            sync_program(sp)

        @block.gpsimd
        def _(pool):
            pool_program(pool, SLABS["end"])

        @block.scalar
        def _(act):
            scalar_program(act)

        @block.tensor
        def _(pe):
            tensor_program(pe)

        @block.vector
        def _(dve):
            vector_program(dve)


_NAMES = ("x", "p", "g_mix", "w_in", "b_gate", "conv_a_w", "conv_a_b", "ln_a_g", "ln_a_b", "w_a_out", "conv_b_w",
          "w_b_out", "w_o", "g_ffn", "w_up", "conv_f_w", "conv_f_b", "w_down", "g_ple", "w_ple", "w_ple_gate",
          "g_final", "c_2", "ctx_2", "c_ctx_2", "w_mod_2", "b_mod_2", "norm_g_2", "w_in_2", "q_lora_g_2", "w_uq_2",
          "kv_lora_g_2", "w_ukv_2", "q_norm_g_2", "k_norm_g_2", "w_pool_2", "pool_scale_2", "w_out_2")


def shape_constants():
    import numpy as np
    pos = np.arange(S)
    inv = (np.float32(10000.0) ** (-np.arange(16, dtype=np.float32) / np.float32(16))).astype(np.float32)
    row = (pos // 64).astype(np.float32)[:, None] * inv
    column = (pos % 64).astype(np.float32)[:, None] * inv
    ang = np.concatenate([row, row, column, column], axis=-1)
    rot = np.zeros((ROPE, ROPE), np.float32)
    for half in (0, 32):
        for j in range(16):
            rot[half + 16 + j, half + j] = -1.0
            rot[half + j, half + 16 + j] = 1.0
    cnt = np.stack([np.clip(pos - w // 2 + w, 0, S) - np.clip(pos - w // 2, 0, S) for w in WINDOWS])
    return {
        "ident": np.eye(P, dtype=np.float32),
        "rotate": rot,
        "rope_cos": np.ascontiguousarray(np.cos(ang).T.astype(np.float32)),
        "rope_sin": np.ascontiguousarray(np.sin(ang).T.astype(np.float32)),
        "inv_cnt": (1.0 / cnt).astype(np.float32),
    }


def kernel(**inputs):
    import numpy as np
    import concourse.bacc as bacc
    from concourse.bass_utils import run_bass_kernel_spmd

    nc = bacc.Bacc("TRN2", target_bir_lowering=False, num_devices=1)
    arrays, A = {}, {}
    for name, a in [(n, inputs[n]) for n in _NAMES] + list(shape_constants().items()):
        a = np.ascontiguousarray(a)
        arrays[f"in_{name}"] = a
        A[name] = nc.dram_tensor(f"in_{name}", a.shape, mybir.dt.from_np(a.dtype), kind="ExternalInput").ap()
    out = nc.dram_tensor("out_x", (1, S, D), F32, kind="ExternalOutput").ap()
    ydram = nc.dram_tensor("y_scratch", (8, P, S), F32, kind="Internal").ap()
    build_program(nc, A, out, ydram)
    r = run_bass_kernel_spmd(nc, [arrays], core_ids=[0])
    return r.results[0]["out_x"]
```

```python
import concourse.bass as bass
from concourse import mybir
from contextlib import ExitStack

F32 = mybir.dt.float32
F32R = mybir.dt.float32r
ALU = mybir.AluOpType
ACT = mybir.ActivationFunctionType
AX = mybir.AxisListType

P = 128
S = 1024
D = 1024
KD = D // P
H = 512
DC = 512
KC = DC // P
TAPS_A, TAPS_B, TAPS_F = 31, 3, 3
DFF = 2816
NF = DFF // P
FC = 2
NCH = NF // FC
PLE = 256
CTX = 256
NKEY = S + CTX
KT = NKEY // P
HEADS, NOPE, ROPE, VD = 4, 128, 64, 128
QH = NOPE + ROPE
EPS = 1e-6
SCALE = QH ** -0.5
WINDOWS = (2, 4, 8, 16)
IN2 = 1984
OFF_CKV, OFF_KR, OFF_GA, OFF_PIN, OFF_GP = 256, 384, 448, 960, 1472

ROWS = [
    [("conv_a_w", 124), ("conv_a_b", 4)],
    [("b_gate", 16), ("ln_a_g", 4), ("ln_a_b", 4), ("conv_b_w", 12), ("g_ffn", 8), ("conv_f_b", 22),
     ("g_ple", 8), ("g_final", 8), ("norm_g_2", 8), ("b_mod_2", 24), ("q_lora_g_2", 2),
     ("kv_lora_g_2", 1), ("pool_scale_2", 4), ("q_norm_g_2", 2), ("k_norm_g_2", 2)],
    [("conv_f_w", 66), ("c_2", 8), ("c_ctx_2", 8)],
]
COL = {}
for _b, _bin in enumerate(ROWS):
    _at = _b * P
    for _name, _n in _bin:
        COL[_name] = _at
        _at += _n

SLABS = {}
_at = 0
for _name, _n in (("glu", 2 * KC), ("short", 3 * KC), ("mix_b", 2 * KD), ("mix_a", 2 * KD), ("wo", KD),
                  ("ffn", 4), ("ffn_loop", 6 * (NCH - 1)), ("ffn_end", 2), ("w_ple", 2), ("ple", KD), ("ga", 4), ("mla_in", 4),
                  ("pin", 4), ("w_pool", 2), ("pool", 4), ("heads", 2 * HEADS), ("out", KD), ("end", 0)):
    SLABS[_name] = _at
    _at += _n
JOBS = {}
_at = 0
for _name, _n in (("x", 8), ("glu", 2 * KC), ("short", 3 * KC), ("mix_b", 2 * KD), ("mix_a", 2 * KD), ("wo", KD),
                  ("ctx", 2), ("p", 2), ("ffn", 4), ("ffn_loop", 12 * (NCH - 1)), ("ffn_end", 8),
                  ("ple", 2 * KD), ("ga", 4), ("mla_in", 6), ("pin", 4), ("pool", 8), ("heads", 6 * HEADS),
                  ("out", KD), ("end", 0)):
    JOBS[_name] = _at
    _at += _n


class Lin:

    def __init__(self, c, n=0, i=0):
        self.c, self.n, self.i = c, n, i

    def __add__(self, k):
        return Lin(self.c + k, self.n, self.i)

    def val(self, k=0):
        return self.c + k + self.n * self.i if self.n else self.c + k

    def half(self):
        return self.c // 2 + (self.n // 2) * self.i if self.n else self.c // 2

    @property
    def slot(self):
        assert self.n % 2 == 0
        return self.c % 2


N_ROW_DMAS = sum(len(b) for b in ROWS) + 2


def ds(i, n=1):
    return bass.ds(i, n)


def build_program(nc, A, out, ydram):
    KB4 = 4096
    TB = 4160

    def at(name, shape, dtype, offset):
        return nc.alloc_sbuf_tensor_at(name, shape, dtype, offset=offset)

    o_raw = 16512
    o_whi = o_raw + 2 * KB4
    o_wlo = o_whi + 2 * KB4
    o_xah = o_wlo + 2 * KB4
    o_xal = o_xah + 8 * KB4
    o_xbh = o_xal + 8 * KB4
    o_xbl = o_xbh + 8 * KB4
    o_r = o_xbl + 8 * KB4
    o_c = o_r + 8 * KB4
    o_t = o_c + 3648
    o_rbc = o_t + 4 * TB
    assert o_rbc + KB4 <= nc.sbuf_usable_end
    raw = at("raw", [P, 2, 1024], F32, o_raw)
    whi = at("whi", [P, 2, 1024], F32R, o_whi)
    wlo = at("wlo", [P, 2, 1024], F32R, o_wlo)
    XAh = at("xa_hi", [P, 8, S], F32R, o_xah)
    XAl = at("xa_lo", [P, 8, S], F32R, o_xal)
    XBh = at("xb_hi", [P, 8, S], F32R, o_xbh)
    XBl = at("xb_lo", [P, 8, S], F32R, o_xbl)
    R = at("resid", [P, 8, S], F32, o_r)
    ident = at("ident", [P, P], F32, o_c)
    ones = at("ones", [P, P], F32, o_c + 512)
    tab = at("tab", [P, 3 * P], F32, o_c + 1024)
    small = at("small", [P, 128], F32, o_c + 2560)
    cs = at("silu_c", [P, KD, 2], F32, o_c + 3072)
    mod_sb = at("mod_sb", [P, 24, 2], F32, o_c + 3200)
    rotm = at("rotm", [ROPE, ROPE], F32, o_c + 3392)
    T = [at(f"t{k}", [P, TB // 4], F32, o_t + k * TB) for k in range(4)]
    rbc = at("rbc", [P, S], F32, o_rbc)
    xn = at("x_nat", [P, 2, D], F32, o_r)
    gbc = at("g_mix_bc", [P, D], F32, o_r + 2 * KB4)
    xs = at("x_scaled", [P, 2, D], F32, o_r + 3 * KB4)
    sqj = at("sq_junk", [P, D], F32, o_r + 5 * KB4)
    rows = at("rows", [P, 3, P], F32, o_r + 6 * KB4)
    LPAD = TAPS_A - 1
    gpad = at("glu_pad", [P, KC, S + LPAD + 2], F32, o_r)
    conv = at("conv_a", [P, KC, S], F32, o_xbl)
    modw = at("w_mod", [P, 3, 2, H], F32, o_r + 5 * KB4)
    modrow = at("mod_row", [2, H], F32, o_r + 17024)
    assert KC * (S + LPAD + 2) * 4 <= 17024 and 17024 + 4 * H <= 5 * KB4
    cstage = at("ctx_nat", [P, 2, D], F32, o_xah + 4 * KB4)
    pstage = at("p_nat", [P, 8, PLE], F32, o_xah + 6 * KB4)
    ctxT = at("ctx_t", [P, KD, CTX], F32, o_xal + 6 * KB4)
    hch = at("hc_hi", [P, KD, CTX], F32R, o_xah + 6 * KB4)
    hcl = at("hc_lo", [P, KD, CTX], F32R, o_xal + 6 * KB4)
    S1 = at("sum_sq", [P, S], F32, o_xah)
    S2 = at("sum_sq_g", [P, S], F32, o_xah + KB4)
    Q1 = at("sq", [P, S], F32, o_xal)
    Q2 = at("sq_g", [P, S], F32, o_xal + KB4)
    wpleh = at("w_ple_hi", [P, 2, D], F32R, o_xah + 2 * KB4)
    wplel = at("w_ple_lo", [P, 2, D], F32R, o_xal + 2 * KB4)
    wpoolh = at("w_pool_hi", [P, 4, P], F32R, o_t + 15360)
    wpooll = at("w_pool_lo", [P, 4, P], F32R, o_t + 15360 + 2048)
    ga = at("silu_gate_a", [P, HEADS, S], F32, o_xal)
    cosb = at("cosb", [ROPE, S], F32, o_xah)
    sinb = at("sinb", [ROPE, S], F32, o_xah + KB4)
    sqck = at("sq_ckv", [P, NKEY], F32, o_xah + 2 * KB4)
    dgck = at("diag_ckv", [P, KT, P], F32, o_xah + 2 * KB4)
    CKh = at("ck_hi", [P, NKEY], F32R, o_r)
    CKl = at("ck_lo", [P, NKEY], F32R, o_r + 5120)
    CQh = at("cq_hi", [P, 2, S], F32R, o_r + 10240)
    CQl = at("cq_lo", [P, 2, S], F32R, o_r + 18432)
    krot = at("k_rot", [ROPE, NKEY], F32, o_r + 26624)
    ckvT = at("ckv_t", [P, NKEY], F32, o_t)
    krT = at("kr_t", [ROPE, NKEY], F32, o_t + 5120)
    sqkr = at("sq_kr", [ROPE, NKEY], F32, o_t + 10240)
    U3 = at("u3", [P, NKEY], F32, o_t + 15360)
    upad = at("u_pad", [P, TB // 4], F32, o_xah)
    wA = at("win_a", [P, TB // 4], F32, o_xah + TB)
    wB = at("win_b", [P, TB // 4], F32, o_xah + 2 * TB)
    inv = at("inv_cnt", [P, S], F32, o_t + 5120)
    pl = at("pooled", [P, S], F32, o_t)
    sgp = at("silu_gate_p", [P, S], F32, o_t + 5120)
    QNh = at("qn_hi", [P, S], F32R, o_xbh)
    QNl = at("qn_lo", [P, S], F32R, o_xbh + 4096)
    QRh = at("qr_hi", [ROPE, S], F32R, o_xbh + 8192)
    QRl = at("qr_lo", [ROPE, S], F32R, o_xbh + 12288)
    KNh = at("kn_hi", [P, NKEY], F32R, o_xbh + 16384)
    KNl = at("kn_lo", [P, NKEY], F32R, o_xbh + 21504)
    KRh = at("kr_hi", [ROPE, NKEY], F32R, o_xbh + 26624)
    KRl = at("kr_lo", [ROPE, NKEY], F32R, o_xbh + 31744)
    Vh = at("v_hi", [P, KT, VD], F32R, o_xbh + 36864)
    Vl = at("v_lo", [P, KT, VD], F32R, o_xbh + 41984)
    Pr = [at(f"prob{k}", [P, NKEY], F32, o_xbh + 47104 + 5120 * k) for k in range(2)]
    cosq = at("cosq", [ROPE, S], F32, o_xbh + 57344)
    sinq = at("sinq", [ROPE, S], F32, o_xbh + 61440)
    PTh = at("pt_hi", [P, KT, 2 * P], F32R, o_xah)
    PTl = at("pt_lo", [P, KT, 2 * P], F32R, o_t)
    dgp = at("diag_p", [P, 2, P], F32, o_xah + KT * 2 * P * 4)
    dgh = at("diag_h", [P, KT, P], F32, o_t)
    dgq = at("q_sin", [ROPE, S], F32, o_t + 5120)
    sqq = at("sq_qr", [ROPE, S], F32, o_xbh + 12288)
    sqk = at("sq_kn", [P, NKEY], F32, o_xbh + 16384)
    ybuf = at("y_back", [P, 8, S], F32, o_xbh)
    yout = at("out_t", [P, 2, S], F32, o_xbl)
    onat = at("out_nat", [P, 2, 8, P], F32, o_xbl + 2 * KB4)
    PS = nc.alloc_psum_tensor("ps", [P, 4096], F32)
    ST, SC, MODB = 2048, 3584, 3072

    sems = {}

    def sem(name):
        if name not in sems:
            sems[name] = nc.alloc_semaphore(name)
        return sems[name]

    def pair(job, a=0, b=1024, p=P):
        return PS[0:p, 1024 * job.slot + a:1024 * job.slot + b]

    def f32(ap):
        return ap.bitcast(F32)

    def col(name, k, p=P):
        return tab[0:p, COL[name] + k:COL[name] + k + 1]

    def dcol(name, k):
        return tab[:, ds(k + COL[name])]

    def tile(x, k, a=0, b=1024):
        if isinstance(k, int):
            return x[:, k, a:b]
        return x[:, ds(k), a:b].rearrange("p o n -> p (o n)")

    raw_in = [sem("raw_in0"), sem("raw_in1")]
    pair_free = [sem("pair_free0"), sem("pair_free1")]
    job_done, split_done, slab_begun = sem("job_done"), sem("split_done"), sem("slab_begun")

    def free(job):
        return pair_free[job.slot], job.half() + 1

    def settle(engine):
        engine.wait_ge(sem("consts_in"), 32)

    def sync_program(sp):
        def load(slab, dst_cols, src, first=False):
            if not first:
                sp.wait_ge(split_done, slab.val(-1))
            sp.dma_start(dst_cols, src).then_inc(raw_in[slab.slot], 16)

        def slab8(slab, w, c, first=False):
            load(slab, raw[:, slab.slot, :].rearrange("p (k n) -> p k n", n=P),
                 w[:, ds(c, P)].rearrange("(k p) n -> p k n", p=P), first)

        def slabk(slab, w, kts, c, n=P, r0=0):
            load(slab, raw[:, slab.slot, 0:kts * n].rearrange("p (k n) -> p k n", n=n),
                 w[ds(r0, kts * P), ds(c, n)].rearrange("(k p) n -> p k n", p=P))

        w_in, w_up, w_down = A["w_in"][0], A["w_up"][0], A["w_down"][0]
        L = Lin(SLABS["glu"])
        sp.dma_start(xn[:, 0, :], A["x"][0, 0:P, :]).then_inc(sem("x_in0"), 16)
        sp.dma_start(gbc[:, :], A["g_mix"][0:1, :].to_broadcast([P, D])).then_inc(sem("g_in"), 16)
        sp.dma_start(xn[:, 1, :], A["x"][0, P:2 * P, :]).then_inc(sem("x_in1"), 16)
        slab8(L, w_in, DC, True)
        slab8(L + 1, w_in, 0, True)
        for t in range(2, 8):
            sp.wait_ge(sem("xs_ready"), t - 1)
            sp.dma_start(xn[:, t % 2, :], A["x"][0, t * P:(t + 1) * P, :]).then_inc(sem(f"x_in{t % 2}"), 16)
        with sp.Fori(2, KC + 1) as i:
            L = Lin(SLABS["glu"] - 2, 2, i)
            slab8(L, w_in, i * P + (DC - P))
            slab8(L + 1, w_in, i * P - P)
        with sp.Fori(1, 3) as q:
            for u in range(2):
                L = Lin(SLABS["short"] + 3 * u - 6, 6, q)
                for k, c in enumerate((1536, 2048, 1024)):
                    slab8(L + k, w_in, q * (2 * P) + (c + (u - 2) * P))
                    for j in (6 * u + 2 * k, 6 * u + 2 * k + 1):
                        sp.wait_ge(sem("modw_free"), q * 12 + (j + 1 - 12))
                        sp.dma_start(modw[:, j % 3, :, :],
                                     A["w_mod_2"][0][2 * P * (j % 4):2 * P * (j % 4 + 1), ds(q * (3 * H) + H * (j // 4 - 3), H)]
                                     .rearrange("(k p) n -> p k n", p=P)).then_inc(sem(f"modw_in{j % 3}"), 16)
        for name, c, w2, a, b, off in (("mix_b", 3584, A["w_b_out"][0], 0, 3, 5), ("mix_b", 3584, A["w_b_out"][0], 3, 8, -3),
                                       ("mix_a", 2560, A["w_a_out"][0], 0, 8, 0)):
            with sp.Fori(a + 1, b + 1) as m:
                L = Lin(SLABS[name] - 2, 2, m)
                slab8(L, w_in, m * P + (c + (off - 1) * P))
                slabk(L + 1, w2, KC, m * P + (off - 1) * P)
        sp.wait_ge(sem("mix_done"), 8)

        def x_columns(u, c):
            sp.dma_start(T[1 + u][:, 0:1024].rearrange("p (t f) -> p t f", f=P),
                         A["x"][0, :, ds(c, P)].rearrange("(t p) f -> p t f", p=P)).then_inc(sem(f"x_in{u}"), 16)

        for u in range(2):
            slab8(Lin(SLABS["wo"] + u), A["w_o"][0], u * P)
            x_columns(u, u * P)
        with sp.Fori(1, KD // 2) as q:
            for u in range(2):
                slab8(Lin(SLABS["wo"] + u, 2, q), A["w_o"][0], q * (2 * P) + u * P)
                sp.wait_ge(sem("xt_pe"), q * 2 + (u - 1))
                x_columns(u, q * (2 * P) + u * P)
        sp.wait_ge(job_done, JOBS["ctx"])
        sp.dma_start(cstage[:, :, :], A["ctx_2"][0].rearrange("(t p) f -> p t f", p=P)).then_inc(sem("ctx_p_in"), 16)
        sp.dma_start(pstage[:, :, :], A["p"][0, 0].rearrange("(t p) f -> p t f", p=P)).then_inc(sem("ctx_p_in"), 16)

        def up_slabs(L, c):
            for k, off in enumerate((0, DFF, P, P + DFF)):
                slab8(L + k, w_up, c * (2 * P) + off)

        def down_slabs(L, c):
            for k in range(2):
                slabk(L + k, w_down, FC, k * H, H, c * (2 * P))

        up_slabs(Lin(SLABS["ffn"]), 0)
        with sp.Fori(0, (NCH - 1) // 2) as q:
            for u in range(2):
                L = Lin(SLABS["ffn_loop"] + 6 * u, 12, q)
                up_slabs(L, q * 2 + (1 + u))
                down_slabs(L + 4, q * 2 + u)
        L = Lin(SLABS["ffn_end"])
        down_slabs(L, NCH - 1)
        for u in range(2):
            slabk(Lin(SLABS["w_ple"] + u), A["w_ple"][0], 2, u * H, H)
        with sp.Fori(0, KD // 2) as q:
            for u in range(2):
                slab8(Lin(SLABS["ple"] + u, 2, q), A["w_ple_gate"][0], q * (2 * P) + u * P)
        w2 = A["w_in_2"][0]
        L = Lin(SLABS["ga"])
        for i in range(4):
            slab8(L + i, w2, OFF_GA + i * P)
        sp.wait_ge(sem("rf_bc"), 1)
        sp.dma_start(cosb[:, :], A["rope_cos"]).then_inc(sem("rope_in"), 16)
        sp.dma_start(sinb[:, :], A["rope_sin"]).then_inc(sem("rope_in"), 16)
        for m in range(8):
            sp.wait_ge(sem("y_ready"), m + 1)
            sp.dma_start(ydram[m], R[:, m, :]).then_inc(sem("y_out"), 16)
        L = Lin(SLABS["mla_in"])
        for k, c in enumerate((OFF_CKV, OFF_KR, 0, P)):
            slab8(L + k, w2, c)
        L = Lin(SLABS["pin"])
        for gq in range(4):
            slab8(L + gq, w2, OFF_PIN + gq * P)
        for u in range(2):
            slab = Lin(SLABS["w_pool"] + u)
            load(slab, raw[:, slab.slot, 0:2 * P].rearrange("p (g n) -> p g n", n=P),
                 A["w_pool_2"][0, 2 * u:2 * u + 2].rearrange("g p n -> p g n"))
        for gq in range(4):
            slab8(Lin(SLABS["pool"] + gq), w2, OFF_GP + gq * P)
        sp.wait_ge(job_done, JOBS["heads"])
        sp.dma_start(cosq[:, :], A["rope_cos"]).then_inc(sem("rope_in"), 16)
        sp.dma_start(sinq[:, :], A["rope_sin"]).then_inc(sem("rope_in"), 16)
        with sp.Fori(0, HEADS) as h:
            L = Lin(SLABS["heads"], 2, h)
            slabk(L, A["w_ukv_2"][0], 1, h * (NOPE + VD), NOPE + VD)
            slabk(L + 1, A["w_uq_2"][0], 2, h * QH, QH)
        L = Lin(SLABS["out"])
        slab8(L, A["w_out_2"][0], 0)
        slab8(L + 1, A["w_out_2"][0], P)
        sp.wait_ge(sem("y_out"), 8 * 16)
        sp.wait_ge(sem("pv_done"), 4 * HEADS)
        for m in range(8):
            sp.dma_start(ybuf[:, m, :], ydram[m]).then_inc(sem("y_in"), 16)
        for m in range(2, 8):
            slab8(L + m, A["w_out_2"][0], m * P)
        for m in range(8):
            sp.wait_ge(sem("on_ready"), m + 1)
            sp.dma_start(out[0, :, m * P:(m + 1) * P].rearrange("(t p) f -> p t f", p=P),
                         onat[:, m % 2, :, :]).then_inc(sem(f"out_done{m % 2}"), 16)
        for k in range(2):
            sp.wait_ge(sem(f"out_done{k}"), 4 * 16)

    def pool_program(pool, n_slabs):
        def split(slab, first=False, lag=0, hi=None, lo=None, n=1024):
            src = raw[:, slab.slot, 0:n]
            if hi is None:
                hi, lo = whi[:, slab.slot, :], wlo[:, slab.slot, :]
            elif len(hi.shape) == 3:
                src = src.rearrange("p (k n) -> p k n", k=hi.shape[1])
            pool.wait_ge(raw_in[slab.slot], (slab.half() + 1) * 16)
            if not first:
                pool.wait_ge(slab_begun, slab.val(-lag))
            nc.gpsimd.tensor_tensor(small[:, 30 + slab.slot:31 + slab.slot], ones[:, 0:1], ones[:, 0:1], ALU.mult)
            nc.gpsimd.tensor_scalar(hi, src, 1.0, 0.0, ALU.mult, ALU.add).then_inc(sem("split_hi"), 1)
            pool.wait_ge(sem("split_hi"), slab.val(1))
            nc.gpsimd.tensor_tensor(lo, src, f32(hi), ALU.subtract).then_inc(split_done, 1)

        pool.wait_ge(sem("consts_set"), 2)
        split(Lin(0), True)
        split(Lin(1), True)
        for begin, end, lag in ((2, SLABS["w_ple"], 0), (SLABS["ple"] + 2, SLABS["w_pool"], 0),
                                (SLABS["pool"], SLABS["heads"] + 2, 0),
                                (SLABS["heads"] + 2, SLABS["out"], 1), (SLABS["out"], n_slabs, 0)):
            if begin == SLABS["ple"] + 2:
                for u in range(2):
                    cols = slice(u * H, u * H + H)
                    split(Lin(SLABS["w_ple"] + u), hi=wpleh[:, :, cols], lo=wplel[:, :, cols])
                pool.wait_ge(sem("ss_done0"), 2)
                for m in range(KD - 2):
                    if m in (3, 5):
                        split(Lin(SLABS["ple"] + m // 5))
                    pool.wait_ge(sem("fx_sq"), m + 9)
                    pool.wait_ge(sem("ss_done"), m + 9)
                    nc.gpsimd.tensor_tensor(rbc[:, :], rbc[:, :], T[1 + 2 * (m % 2)][:, 0:S], ALU.add).then_inc(sem("ss_done"), 1)
            if begin == SLABS["pool"]:
                pool.wait_ge(sem("krot_done"), 3)
                for u in range(2):
                    split(Lin(SLABS["w_pool"] + u), hi=wpoolh[:, 2 * u:2 * u + 2, :], lo=wpooll[:, 2 * u:2 * u + 2, :], n=2 * P)
            with pool.Fori(begin // 2, end // 2) as q:
                split(Lin(0, 2, q))
                split(Lin(1, 2, q), lag=lag)

    def tensor_program(pe):
        mm = nc.tensor.matmul

        def split_products(dst, whk, wlk, rhk, rlk, first, last, begun=None):
            n = len(dst)
            done = None
            for w, r, f, l in ((whk, rhk, True, False), (whk, rlk, False, False), (wlk, rhk, False, True)):
                for j in range(n):
                    ins = mm(dst[j], w, r[j], start=first and f, stop=last and l)
                    if begun is not None:
                        ins.then_inc(slab_begun, begun)
                        begun = None
                    done = ins
            return done

        def gemm(job, slab, rh, rl, kts, wcol, new_slab=True, n=1024, each_k=None, waited=KD, order=None,
                 col0=0, p=P, begins=1, weights=None):
            if job.n or job.c >= 2:
                pe.wait_ge(pair_free[job.slot], job.half())
            if new_slab:
                pe.wait_ge(split_done, slab.val(1))
            cuts = [(a, min(a + H, n)) for a in range(0, n, H)]
            order = order or range(kts)
            for k in order:
                if each_k is not None and k < waited:
                    pe.wait_ge(each_k[0], each_k[1] + (k + 1))
                if weights is None:
                    w = slice(wcol(k), wcol(k) + P)
                    wh, wl = whi[0:p, slab.slot, w], wlo[0:p, slab.slot, w]
                else:
                    wh, wl = (x[0:p, wcol(k)[0], wcol(k)[1]] for x in weights)
                last = split_products(
                    [pair(job, a, b) for a, b in cuts], wh, wl,
                    [rh[0:p, k, col0 + a:col0 + b] for a, b in cuts],
                    [rl[0:p, k, col0 + a:col0 + b] for a, b in cuts],
                    k == order[0], k == order[-1], begins if new_slab and k == order[0] else None)
            last.then_inc(job_done, 1)

        def w8(k):
            return k * P

        def transposes(job, srcs):
            if job.n or job.c >= 2:
                pe.wait_ge(pair_free[job.slot], job.half())
            for j, src in enumerate(srcs):
                last = nc.tensor.transpose(pair(job, j * P, j * P + P), src, ident[:, :])
            last.then_inc(job_done, 1)

        def column_sums(src, n, at_col, ready, count):
            pe.wait_ge(ready, count)
            for t in range(n):
                last = mm(PS[:, SC + at_col + t:SC + at_col + t + 1], src[:, t * P:(t + 1) * P],
                          ones[:, 0:1], start=True, stop=True)
            last.then_inc(sem("cols_pe"), 1)

        def broadcast(dg, n, count):
            pe.wait_ge(sem("diag"), count)
            d = dg.rearrange("p t n -> p (t n)")
            for a in range(0, n * P, H):
                b = min(a + H, n * P)
                last = mm(PS[:, ST + a:ST + b], ones[:, :], d[:, a:b], start=True, stop=True)
            last.then_inc(sem("bc_pe"), 1)

        pe.wait_ge(sem("consts_in"), 32)
        for t in range(8):
            pe.wait_ge(sem("xs_ready"), t + 1)
            transposes(Lin(JOBS["x"] + t), [xs[:, t % 2, k * P:(k + 1) * P] for k in range(KD)])
        pe.wait_ge(sem("rows_in"), N_ROW_DMAS * 16)
        for b in range(3):
            last = nc.tensor.transpose(PS[:, ST + b * P:ST + (b + 1) * P], rows[:, b, :], ident[:, :])
        last.then_inc(sem("tab_pe"), 1)
        pe.wait_ge(sem("cs"), 2)
        pe.wait_ge(pair_free[0], 4)
        pe.wait_ge(pair_free[1], 4)
        with pe.Fori(0, KC) as i:
            J, L = Lin(JOBS["glu"], 2, i), Lin(SLABS["glu"], 2, i)
            gemm(J, L, XAh, XAl, KD, w8)
            gemm(J + 1, L + 1, XAh, XAl, KD, w8)
        with pe.Fori(0, 2) as q:
            for k in range(6):
                for j in (2 * k, 2 * k + 1):
                    pe.wait_ge(sem(f"modw_in{j % 3}"), q * 64 + 16 * (j // 3 + 1))
                    for n in range(2):
                        last = mm(PS[0:2, MODB:MODB + H], cs[:, 2 * (j % 4) + n, :], modw[:, j % 3, n, :],
                                  start=j % 4 == 0 and n == 0, stop=j % 4 == 3 and n == 1)
                    last.then_inc(sem("modw_free"), 1)
                if k % 2 == 1:
                    pe.wait_ge(sem("mod_read"), q * 3 + (k // 2 + 1))
                gemm(Lin(JOBS["short"] + k, 6, q), Lin(SLABS["short"] + k, 6, q), XAh, XAl, KD, w8)
                if k % 2 == 1:
                    settle(pe)
                    pe.wait_ge(sem("mod_row"), q * 3 + (k // 2 + 1))
                    for j in range(4):
                        last = nc.tensor.transpose(PS[:, SC + 64 + 2 * j:SC + 66 + 2 * j],
                                                   modrow[:, j * P:(j + 1) * P], ident[0:2, 0:2])
                    last.then_inc(sem("mod_pe"), 1)

        def mix_turns(name, rh, rl, a, b):
            with pe.Fori(a, b) as m:
                J, L = Lin(JOBS[name], 2, m), Lin(SLABS[name], 2, m)
                gemm(J, L, XAh, XAl, KD, w8)
                gemm(J + 1, L + 1, rh, rl, KC, w8)

        pe.wait_ge(sem("branch_lo"), 4)
        mix_turns("mix_b", XBh[:, 4:8, :], XBl[:, 4:8, :], 0, 3)
        pe.wait_ge(sem("ln_v"), 3)
        for a in (0, H):
            last = mm(PS[:, ST + a:ST + a + H], ones[:, :], T[1][:, a:a + H], start=True, stop=True)
        last.then_inc(sem("ln_pe"), 1)
        mix_turns("mix_b", XBh[:, 4:8, :], XBl[:, 4:8, :], 3, 5)
        column_sums(T[1], 8, 0, sem("ln_v"), 10)
        mix_turns("mix_b", XBh[:, 4:8, :], XBl[:, 4:8, :], 5, 7)
        broadcast(T[2][:, 0:1024].rearrange("p (t n) -> p t n", n=P), 8, 1)
        mix_turns("mix_b", XBh[:, 4:8, :], XBl[:, 4:8, :], 7, 8)
        J, L = Lin(JOBS["mix_a"]), Lin(SLABS["mix_a"])
        gemm(J, L, XAh, XAl, KD, w8)
        pe.wait_ge(sem("branch_lo"), 8)
        gemm(J + 1, L + 1, XBh[:, 0:4, :], XBl[:, 0:4, :], KC, w8)
        mix_turns("mix_a", XBh[:, 0:4, :], XBl[:, 0:4, :], 1, 8)

        def wo_job(J, L, m, u, each_k=None):
            pe.wait_ge(sem(f"x_in{u}"), (m // 2 if isinstance(m, int) else m[0]) * 16 + 5 * 16)
            if isinstance(m, tuple) or m >= 1:
                pe.wait_ge(sem("xt_sb"), m if isinstance(m, int) else m[1])
            for t in range(8):
                last = nc.tensor.transpose(PS[:, ST + t * P:ST + (t + 1) * P], T[1 + u][:, t * P:(t + 1) * P], ident[:, :])
            last.then_inc(sem("xt_pe"), 1)
            gemm(J, L, XAh, XAl, KD, w8, each_k=each_k)

        for m in range(2):
            wo_job(Lin(JOBS["wo"] + m), Lin(SLABS["wo"] + m), m, m, (sem("mx_lo"), 0) if m == 0 else None)
        with pe.Fori(1, KD // 2) as q:
            for u in range(2):
                wo_job(Lin(JOBS["wo"] + u, 2, q), Lin(SLABS["wo"] + u, 2, q), (q, q * 2 + u), u)
        for t in range(2):
            pe.wait_ge(sem("cs_ready"), t + 1)
            transposes(Lin(JOBS["ctx"] + t), [cstage[:, t, k * P:(k + 1) * P] for k in range(KD)])
        for k in range(2):
            pe.wait_ge(sem("ctx_p_in"), 32)
            transposes(Lin(JOBS["p"] + k), [pstage[:, t, k * P:(k + 1) * P] for t in range(8)])

        def ffn_down(J, L, slot, begins=1):
            for m in range(KD):
                gemm(J + m, L + m // 4, XAh[:, 2 * slot:2 * slot + 2, :], XAl[:, 2 * slot:2 * slot + 2, :], FC,
                     lambda k: k * H + (m % 4) * P, new_slab=m % 4 == 0, begins=begins if m == 0 else 1)

        J, L = Lin(JOBS["ffn"]), Lin(SLABS["ffn"])
        pe.wait_ge(sem("fx_lo"), 8)
        for k in range(2):
            gemm(J + k, L + k, XBh, XBl, KD, w8)
        column_sums(rbc, 8, 0, sem("ss_done"), 9)
        broadcast(T[3][:, 0:1024].rearrange("p (t n) -> p t n", n=P), 8, 2)
        for k in range(2, 4):
            gemm(J + k, L + k, XBh, XBl, KD, w8)
        with pe.Fori(0, (NCH - 1) // 2) as q:
            for u in range(2):
                J, L = Lin(JOBS["ffn_loop"] + 12 * u, 24, q), Lin(SLABS["ffn_loop"] + 6 * u, 12, q)
                for k in range(4):
                    gemm(J + k, L + k, XBh, XBl, KD, w8)
                pe.wait_ge(sem("f_lo"), q * 4 + (2 * u + 2))
                ffn_down(J + 4, L + 4, u)
        J, L = Lin(JOBS["ffn_end"]), Lin(SLABS["ffn_end"])
        pe.wait_ge(sem("f_lo"), 2 * NCH)
        ffn_down(J, L, (NCH - 1) % 2, 3)

        def p_product(J, m):
            gemm(J, None, XAh[:, 4:6, :], XAl[:, 4:6, :], 2, lambda k: (k, slice(m * P, m * P + P)), new_slab=False,
                 weights=(wpleh, wplel))

        J, L = Lin(JOBS["ple"]), Lin(SLABS["ple"])
        gemm(J, L, XBh, XBl, KD, w8, each_k=(sem("fx_lo"), 8))
        column_sums(rbc, 8, 0, sem("ss_done"), KD + 8)
        p_product(J + 1, 0)
        broadcast(T[3][:, 0:1024].rearrange("p (t n) -> p t n", n=P), 8, 3)
        for m in range(1, KD):
            gemm(J + 2 * m, L + m, XBh, XBl, KD, w8)
            p_product(J + (2 * m + 1), m)
        column_sums(S1, 8, 0, sem("s12_done"), 18)
        column_sums(S2, 8, 8, sem("s12_done"), 18)
        broadcast(Q1[:, :].rearrange("p (t n) -> p t n", n=P), 8, 4)
        pe.wait_ge(sem("rh_bc"), 1)
        broadcast(Q2[:, :].rearrange("p (t n) -> p t n", n=P), 8, 5)
        J, L = Lin(JOBS["ga"]), Lin(SLABS["ga"])
        for i in range(4):
            gemm(J + i, L + i, XBh, XBl, KD, w8, each_k=(sem("h_lo"), 0) if i == 0 else None)
        J, L = Lin(JOBS["mla_in"]), Lin(SLABS["mla_in"])
        pe.wait_ge(sem("h_lo"), 9)
        for k in range(2):
            gemm(J + 2 * k, L + k, XBh, XBl, KD, w8)
            gemm(J + (2 * k + 1), L + k, hch, hcl, KD, w8, new_slab=False, n=CTX)
        for k in range(2):
            gemm(J + (4 + k), L + (2 + k), XBh, XBl, KD, w8)
        pe.wait_ge(sem("kr_sb"), 2)
        for a in (0, H):
            last = mm(PS[0:ROPE, ST + a:ST + a + H], rotm[:, :], krT[:, a:a + H], start=True, stop=True)
        last.then_inc(sem("rot_pe"), 1)
        column_sums(sqck, KT, 0, sem("ck_sq"), 2)
        J, L = Lin(JOBS["pin"]), Lin(SLABS["pin"])
        gemm(J, L, XBh, XBl, KD, w8)
        pe.wait_ge(sem("krot_mul"), 1)
        broadcast(dgck[:, :, :], KT, 6)
        column_sums(cqs[:, 0, :], 8, 16, sem("cq_ss"), 1)
        for gq in range(1, 4):
            gemm(J + gq, L + gq, XBh, XBl, KD, w8, begins=3 if gq == 2 else 1)
        J, L = Lin(JOBS["pool"]), Lin(SLABS["pool"])
        for gq in range(4):
            gemm(J + 2 * gq, L + gq, XBh, XBl, KD, w8)
            pe.wait_ge(sem("pool_lo"), gq + 1)
            gemm(J + (2 * gq + 1), None, XAh[:, 4 + gq:5 + gq, :], XAl[:, 4 + gq:5 + gq, :], 1,
                 lambda k: (gq, slice(0, P)), new_slab=False, weights=(wpoolh, wpooll))

        CKh3, CKl3 = CKh[:, :].unsqueeze(1), CKl[:, :].unsqueeze(1)
        pe.wait_ge(sem("ck_lo"), 1)
        pe.wait_ge(sem("cq_lo"), 2)
        with pe.Fori(0, HEADS) as h:
            J, L = Lin(JOBS["heads"], 6, h), Lin(SLABS["heads"], 2, h)
            gemm(J, L, CKh3, CKl3, 1, w8)
            pe.wait_ge(split_done, (L + 1).val(1))
            gemm(J + 1, L + 1, CQh, CQl, 2, lambda k: k * QH + NOPE, new_slab=False)
            pe.wait_ge(sem("qr_sb"), h + 1)
            gemm(J + 2, L, CKh3, CKl3, 1, w8, new_slab=False, n=CTX, col0=S)
            for a in (0, H):
                last = mm(PS[0:ROPE, ST + a:ST + a + H], rotm[:, :], U3[0:ROPE, a:a + H], start=True, stop=True)
            last.then_inc(sem("qrot_pe"), 1)
            pe.wait_ge(*free(J + 1))
            for t in range(8):
                last = mm(PS[:, SC + 48 + t:SC + 49 + t], sqq[:, t * P:(t + 1) * P], ones[0:ROPE, 0:1], start=True, stop=True)
            last.then_inc(sem("qcols"), 1)
            pe.wait_ge(sem("k_ss"), h + 2)
            for t in range(KT):
                last = mm(PS[:, SC + t:SC + t + 1], sqk[:, t * P:(t + 1) * P], ones[:, 0:1], start=True, stop=True)
            last.then_inc(sem("kcols"), 1)

            def v_product(job, t0, t1):
                wv = slice(NOPE, NOPE + VD)
                pe.wait_ge(pair_free[job.slot], job.half())
                for t in range(t0, t1):
                    k = slice(t * P, (t + 1) * P)
                    o = pair(job, (t - t0) * P, (t - t0 + 1) * P)
                    mm(o, CKh[:, k], whi[:, L.slot, wv], start=True, stop=False)
                    mm(o, CKh[:, k], wlo[:, L.slot, wv], start=False, stop=False)
                    last = mm(o, CKl[:, k], whi[:, L.slot, wv], start=False, stop=True)
                last.then_inc(job_done, 1)

            gemm(J + 3, L + 1, CQh, CQl, 2, lambda k: k * QH, new_slab=False)
            pe.wait_ge(sem("kdiag"), h + 1)
            pe.wait_ge(sem("qr_a"), h * 2 + 1)
            d = dgh[:, :, :].rearrange("p t n -> p (t n)")
            for a in range(0, NKEY, H):
                b = min(a + H, NKEY)
                last = mm(PS[:, ST + a:ST + b], ones[:, :], d[:, a:b], start=True, stop=True)
            last.then_inc(sem("kbc"), 1)
            v_product(J + 4, 0, 8)
            v_product(J + 5, 8, KT)
            pe.wait_ge(sem("qn_sq"), h + 1)
            for t in range(8):
                last = mm(PS[:, SC + 16 + t:SC + 17 + t], Pr[1][:, t * P:(t + 1) * P], ones[:, 0:1], start=True, stop=True)
            last.then_inc(sem("qcols"), 1)
            pe.wait_ge(sem("kr_lo"), h + 1)
            pe.wait_ge(sem("v_lo"), h * 2 + 2)

            def scores(t, begun=None):
                if t >= 2:
                    pe.wait_ge(sem("pt_lo"), h * 24 + 3 * (t - 1))
                q = slice(t * P, (t + 1) * P)
                terms = ((QNh, KNh), (QNh, KNl), (QNl, KNh), (QRh, KRh), (QRh, KRl), (QRl, KRh))
                for n_, (ql, kr_) in enumerate(terms):
                    for c0 in range(0, NKEY, H):
                        c1 = min(c0 + H, NKEY)
                        last = mm(PS[:, 1536 * (t % 2) + c0:1536 * (t % 2) + c1], ql[:, q], kr_[:, c0:c1],
                                  start=n_ == 0, stop=n_ == 5)
                        if begun is not None:
                            last.then_inc(begun, 1)
                            begun = None
                last.then_inc(sem("s_done"), 1)

            scores(0, slab_begun)
            scores(1)
            for g in range(4):
                for t in (2 * g, 2 * g + 1):
                    pe.wait_ge(sem("p_diag"), h * 8 + (t + 1))
                    for k0, k1 in ((0, 4), (4, 8), (8, 10)):
                        for k in range(k0, k1):
                            o = 1536 * (t % 2) + k * P
                            last = mm(PS[:, o:o + P], Pr[t % 2][:, k * P:(k + 1) * P], dgp[:, t % 2, :],
                                      start=True, stop=True)
                        last.then_inc(sem("pt_pe"), 1)
                if g < 3:
                    scores(2 * g + 2)
                    scores(2 * g + 3)
                pe.wait_ge(sem("pt_lo"), h * 24 + (6 * g + 6))
                if g >= 1:
                    pe.wait_ge(sem("o_read"), h * 4 + g)
                o = PS[:, 3072:3072 + 2 * P]
                for k in range(KT):
                    mm(o, Vh[:, k, :], PTh[:, k, :], start=k == 0, stop=False)
                    mm(o, Vh[:, k, :], PTl[:, k, :], start=False, stop=False)
                    last = mm(o, Vl[:, k, :], PTh[:, k, :], start=False, stop=k == KT - 1)
                last.then_inc(sem("pv_done"), 1)
            pe.wait_ge(sem("o_read"), h * 4 + 4)

        J, L = Lin(JOBS["out"]), Lin(SLABS["out"])
        for m in range(9):
            if m < 8:
                gemm(J + m, L + m, XAh, XAl, KD, w8, each_k=(sem("br_lo"), 0) if m == 0 else None, waited=4,
                     order=(4, 5, 6, 7, 0, 1, 2, 3))
            if m >= 1:
                u = m - 1
                pe.wait_ge(sem("yo_ready"), u + 1)
                if u >= 1:
                    pe.wait_ge(sem("on_ready"), u)
                for t in range(8):
                    last = nc.tensor.transpose(PS[:, ST + t * P:ST + (t + 1) * P], yout[:, u % 2, t * P:(t + 1) * P], ident[:, :])
                last.then_inc(sem("yt_pe"), 1)

    def one(f):
        return f[0], 1

    cqs = at("sq_cq", [P, 2, S], F32, o_xah + 4 * KB4)
    var, sd, rcp = small[:, 0:16], small[:, 16:32], small[:, 32:48]
    ssq, csq = small[:, 48:56], small[:, 56:58]
    Gx, Gc, gfn = small[:, 64:72], small[:, 72:80], small[:, 80:88]
    rql, rqs = small[:, 88:96], small[:, 96:104]
    eps_col = small[:, 64:65]
    mx, rsum, nbias = small[:, 104:106], small[:, 106:108], small[:, 108:110]
    tmp8, tmp8b = small[:, 110:118], small[:, 118:126]

    def scalar_program(act):
        fn = nc.scalar.activation

        def root(n, count):
            act.wait_ge(sem("var"), count)
            fn(sd[:, 0:n], var[:, 0:n], ACT.Sqrt).then_inc(sem("sd"), 1)

        act.dma_start(ident[:, :], A["ident"]).then_inc(sem("consts_in"), 16)
        act.dma_start(rotm[:, :], A["rotate"]).then_inc(sem("consts_in"), 16)
        act.wait_ge(sem("consts_set"), 1)
        for b, bin_ in enumerate(ROWS):
            r = 0
            for name, n in bin_:
                src = A[name]
                if name in ("q_norm_g_2", "k_norm_g_2"):
                    act.dma_start(rows[r:r + 1, b, :], src[0:1, 0:P]).then_inc(sem("rows_in"), 16)
                    act.dma_start(rows[r + 1:r + 2, b, 0:ROPE], src[0:1, P:QH]).then_inc(sem("rows_in"), 16)
                else:
                    if len(src.shape) == 3:
                        flat = src.rearrange("a k (n p) -> (a k n) p", p=P)
                    elif len(src.shape) == 2:
                        flat = src.rearrange("a (n p) -> (a n) p", p=P)
                    else:
                        flat = src.rearrange("(n p) -> n p", p=P)
                    act.dma_start(rows[r:r + n, b, :], flat).then_inc(sem("rows_in"), 16)
                r += n
        for t in range(9):
            if t < 8:
                act.wait_ge(sem(f"x_in{t % 2}"), 16 * (t // 2 + 1))
                fn(sqj[:, :], xn[:, t % 2, :], ACT.Square, accum_out=ssq[:, t:t + 1]).then_inc(sem("n1_sq"), 1)
                act.wait_ge(sem("row_var"), t + 1)
                fn(sd[:, t:t + 1], var[:, t:t + 1], ACT.Sqrt).then_inc(sem("row_sd"), 1)
            if t >= 1:
                J = Lin(JOBS["x"] + t - 1)
                act.wait_ge(job_done, J.val(1))
                fn(XAh[:, :, (t - 1) * P:t * P], pair(J).rearrange("p (m n) -> p m n", n=P), ACT.Copy).then_inc(sem("x_hi"), 1)
        act.wait_ge(sem("tab_ready"), 1)
        for k, name in enumerate(("c_2", "c_ctx_2")):
            fn(cs[:, :, k], tab[:, COL[name]:COL[name] + KD], ACT.Silu).then_inc(sem("cs"), 1)
        with act.Fori(0, KC) as i:
            J = Lin(JOBS["glu"], 2, i)
            act.wait_ge(job_done, J.val(1))
            act.wait_ge(pair_free[(J + 1).slot], (J + 1).half())
            fn(T[0][:, 0:S], pair(J), ACT.Sigmoid).then_inc(*one(free(J)))
        act.wait_ge(*free(Lin(JOBS["short"] - 1)))
        with act.Fori(0, 2) as q:
            for u in range(2):
                J = Lin(JOBS["short"] + 3 * u, 6, q)
                act.wait_ge(job_done, J.val(1))
                act.wait_ge(sem("cv_ready"), q * 2 + (u + 1))
                fn(T[0][:, 0:S], pair(J), ACT.Copy).then_inc(*one(free(J)))
                for g in ((0, 1), (2,))[u]:
                    act.wait_ge(sem("modw_free"), q * 12 + (4 * g + 7))
                    if g > 0:
                        act.wait_ge(sem("mod_pe"), q * 3 + g)
                    fn(modrow[:, :], PS[0:2, MODB:MODB + H], ACT.Copy).then_inc(sem("mod_row"), 1)
                act.wait_ge(sem("s_ready"), q * 2 + (u + 1))
                fn(tile(XBh, q * 2 + (4 + u)), T[3][:, 0:S], ACT.Copy).then_inc(sem("branch_hi"), 1)

        def gate_sigmoid(name, a, b, c0):
            with act.Fori(a, b) as m:
                J = Lin(JOBS[name], 2, m)
                act.wait_ge(job_done, J.val(1))
                act.wait_ge(pair_free[1], (J + 1).half())
                fn(T[0][:, 0:S], pair(J), ACT.Sigmoid, bias=dcol("b_gate", m + c0)).then_inc(*one(free(J)))

        gate_sigmoid("mix_b", 0, 3, 8 + 5)
        for i in range(4):
            act.wait_ge(sem("ln_v"), 4 + i)
            if i >= 2:
                act.wait_ge(sem("ln_v"), 8)
            fn(T[2 + i % 2][:, 0:S], conv[:, i, :], ACT.Square).then_inc(sem("ln_sq"), 1)
        gate_sigmoid("mix_b", 3, 5, 8 - 3)
        root(8, 1)
        gate_sigmoid("mix_b", 5, 7, 8 - 3)
        act.wait_ge(sem("bc_pe"), 1)
        fn(rbc[:, :], PS[:, ST:ST + S], ACT.Copy).then_inc(sem("rbc_ready"), 1)
        for i in range(4):
            act.wait_ge(sem("ln_n"), i + 1)
            if i >= 1:
                act.wait_ge(sem("branch_lo"), 4 + i)
            fn(T[3][:, 0:S], T[1 + i % 2][:, 0:S], ACT.Silu, scale=col("ln_a_g", i), bias=col("ln_a_b", i)).then_inc(sem("a_silu"), 1)
            act.wait_ge(sem("a_silu"), i + 1)
            fn(XBh[:, i, :], T[3][:, 0:S], ACT.Copy).then_inc(sem("branch_hi"), 1)
        gate_sigmoid("mix_b", 7, 8, 8 - 3)
        gate_sigmoid("mix_a", 0, 8, 0)
        for m in range(8):
            act.wait_ge(sem("mix_done"), m + 1)
            if m == 0:
                act.wait_ge(job_done, JOBS["wo"])
            fn(XAh[:, m, :], R[:, m, :], ACT.Copy).then_inc(sem("mx_hi"), 1)

        with act.Fori(0, KD // 2) as q:
            for u in range(2):
                J = Lin(JOBS["wo"] + u, 2, q)
                m = q * 2 + u
                act.wait_ge(sem("xt_pe"), q * 2 + (u + 1))
                act.wait_ge(sem("x2_ready"), q * 2 + (u + 1))
                fn(T[0][:, 0:S], PS[:, ST:ST + S], ACT.Copy).then_inc(sem("xt_sb"), 1)
                act.wait_ge(pair_free[u], (J + 0).half() + 1)
                fn(tile(XBh, m), tile(R, m), ACT.Copy, scale=dcol("g_ffn", m)).then_inc(sem("fx_hi"), 1)
                settle(act)
                act.wait_ge(sem("ss_done"), q * 2 + (u + 1))
                fn(T[3][:, 0:S], tile(R, m), ACT.Square).then_inc(sem("fx_sq"), 1)
        act.wait_ge(sem("x2_ready"), 9)
        for t in range(2):
            act.wait_ge(sem("ctx_p_in"), 32)
            if t == 1:
                act.wait_ge(sem("c_sq"), 1)
            fn(T[0][:, 0:S], cstage[:, t, :], ACT.Square, accum_out=csq[:, t:t + 1]).then_inc(sem("c_sq"), 1)
        act.wait_ge(sem("row_var"), 9)
        fn(sd[:, 0:2], var[:, 0:2], ACT.Sqrt).then_inc(sem("row_sd"), 1)
        for t in range(2):
            J = Lin(JOBS["ctx"] + t)
            act.wait_ge(job_done, J.val(1))
            fn(ctxT[:, :, t * P:(t + 1) * P], pair(J).rearrange("p (m n) -> p m n", n=P), ACT.Copy).then_inc(*one(free(J)))
        for k in range(2):
            J = Lin(JOBS["p"] + k)
            act.wait_ge(job_done, J.val(1))
            fn(XAh[:, 4 + k, :], pair(J), ACT.Copy).then_inc(sem("pt_hi"), 1)
        root(8, 2)
        act.wait_ge(sem("bc_pe"), 2)
        act.wait_ge(sem("cols_pe"), 2)
        fn(rbc[:, :], PS[:, ST:ST + S], ACT.Copy).then_inc(sem("rbc_ready"), 1)

        def ffn_chunk(n, slot):
            for k in range(2):
                act.wait_ge(sem("fc_tap"), n * 3 + (3 * k + 3))
                fn(T[2][:, 0:S], T[1][:, 0:S], ACT.Gelu_apprx_tanh).then_inc(sem("gelu"), 1)
                act.wait_ge(sem("f_ready"), n + (k + 1))
                fn(XAh[:, 2 * slot + k, :], T[3][:, 0:S], ACT.Copy).then_inc(sem("f_hi"), 1)

        ffn_chunk(0, 0)
        with act.Fori(0, (NCH - 1) // 2) as q:
            for u in range(2):
                ffn_chunk(q * 4 + (2 * u + 2), 1 - u)
        for m in range(KD):
            act.wait_ge(*free(Lin(JOBS["ffn_end"] + m)))
            fn(XBh[:, m, :], R[:, m, :], ACT.Copy, scale=col("g_ple", m)).then_inc(sem("fx_hi"), 1)
            act.wait_ge(sem("f_lo"), 2 * NCH)
            if m >= 2:
                act.wait_ge(sem("ss_done"), m + 8)
            fn(T[1 + 2 * (m % 2)][:, 0:S], R[:, m, :], ACT.Square).then_inc(sem("fx_sq"), 1)
        root(8, 3)
        act.wait_ge(sem("bc_pe"), 3)
        fn(rbc[:, :], PS[:, ST:ST + S], ACT.Copy).then_inc(sem("rbc_ready"), 1)
        with act.Fori(0, KD) as m:
            act.wait_ge(*free(Lin(JOBS["ple"], 2, m)))
            fn(T[1][:, 0:S], T[0][:, 0:S], ACT.Sigmoid).then_inc(sem("pg_sig"), 1)
            settle(act)
            act.wait_ge(sem("x4_ready"), m + 1)
            act.wait_ge(sem("s12_done"), m * 2 + 2)
            fn(Q1[:, :], tile(R, m), ACT.Square).then_inc(sem("q12"), 1)
            fn(Q2[:, :], tile(R, m), ACT.Square, scale=dcol("g_final", m)).then_inc(sem("q12"), 1)
        root(8, 4)
        root(8, 5)
        act.wait_ge(sem("bc_pe"), 4)
        fn(rbc[:, :], PS[:, ST:ST + S], ACT.Copy).then_inc(sem("rh_bc"), 1)
        act.wait_ge(sem("bc_pe"), 5)
        fn(T[3][:, 0:S], PS[:, ST:ST + S], ACT.Copy).then_inc(sem("rf_bc"), 1)
        for m in range(8):
            act.wait_ge(sem("h_n"), m + 1)
            if m >= 1:
                act.wait_ge(sem("h_lo"), m)
            fn(T[2][:, 0:S], T[m % 2][:, 0:S], ACT.Identity, scale=Gx[:, m:m + 1], bias=mod_sb[:, m, 0:1]).then_inc(sem("h_f"), 1)
            act.wait_ge(sem("h_f"), m + 1)
            fn(XBh[:, m, :], T[2][:, 0:S], ACT.Copy).then_inc(sem("h_hi"), 1)
        for m in range(8):
            fn(ctxT[:, m, :], ctxT[:, m, :], ACT.Identity, scale=Gc[:, m:m + 1], bias=mod_sb[:, m, 1:2]).then_inc(sem("hc_f"), 1)
        act.wait_ge(sem("hc_f"), 8)
        fn(hch[:, :, :], ctxT[:, :, :], ACT.Copy).then_inc(sem("h_hi"), 1)
        for i in range(4):
            J = Lin(JOBS["ga"] + i)
            act.wait_ge(job_done, J.val(1))
            fn(ga[:, i, :], pair(J), ACT.Silu).then_inc(*one(free(J)))
        J = Lin(JOBS["mla_in"])
        for k, (j, a, b) in enumerate(((J, 0, S), (J + 1, S, NKEY))):
            act.wait_ge(job_done, j.val(1))
            if k == 0:
                act.wait_ge(sem("y_ready"), 8)
            fn(sqck[:, a:b], pair(j, 0, b - a), ACT.Square).then_inc(sem("ck_sq"), 1)
            fn(ckvT[:, a:b], pair(j, 0, b - a), ACT.Copy).then_inc(*one(free(j)))
        for k, (j, a, b) in enumerate(((J + 2, 0, S), (J + 3, S, NKEY))):
            act.wait_ge(job_done, j.val(1))
            fn(sqkr[:, a:b], pair(j, 0, b - a, ROPE), ACT.Square).then_inc(sem("kr_sq"), 1)
            fn(krT[:, a:b], pair(j, 0, b - a, ROPE), ACT.Copy, scale=col("k_norm_g_2", 1, ROPE)).then_inc(sem("kr_sb"), 1)
        for k in range(2):
            j = J + (4 + k)
            act.wait_ge(job_done, j.val(1))
            fn(cqs[:, k, :], pair(j), ACT.Square).then_inc(sem("cq_sq"), 1)
            if k == 0:
                act.wait_ge(sem("y_out"), 8 * 16)
            fn(CQh[:, k, :], pair(j), ACT.Copy, scale=col("q_lora_g_2", k)).then_inc(sem("cq_hi"), 1)
        root(KT, 6)
        act.wait_ge(sem("ck_f"), 1)
        fn(CKh[:, :], ckvT[:, :], ACT.Copy).then_inc(sem("ck_hi"), 1)
        for gq in range(4):
            J = Lin(JOBS["pin"] + gq)
            if gq == 0:
                act.wait_ge(sem("krot_done"), 3)
                act.wait_ge(sem("pads2_zero"), 3)
            else:
                act.wait_ge(sem("pool_ready"), gq)
            act.dma_start(inv[:, :], A["inv_cnt"][gq:gq + 1, :].to_broadcast([P, S])).then_inc(sem("inv_in"), 16)
            act.wait_ge(job_done, J.val(1))
            fn(upad[:, 8:8 + S], pair(J), ACT.Copy).then_inc(*one(free(J)))
            act.wait_ge(sem("pool_ready"), gq + 1)
            if gq == 0:
                act.wait_ge(sem("cols_pe"), 7)
            fn(XAh[:, 4 + gq, :], pl[:, :], ACT.Copy).then_inc(sem("pool_hi"), 1)
            if gq == 0:
                root(8, 7)
        for gq in range(4):
            J = Lin(JOBS["pool"] + 2 * gq)
            act.wait_ge(job_done, J.val(1))
            if gq >= 1:
                act.wait_ge(sem("pool_ready"), 4 + gq)
            fn(sgp[:, :], pair(J), ACT.Silu).then_inc(*one(free(J)))
            act.wait_ge(sem("pool_ready"), 4 + gq + 1)
            fn(XAh[:, 4 + gq, :], pl[:, :], ACT.Copy).then_inc(sem("pool_hi"), 1)
        act.wait_ge(sem("pool_lo"), 8)
        with act.Fori(0, HEADS) as h:
            J = Lin(JOBS["heads"], 6, h)
            act.wait_ge(*free(J))
            fn(sqk[:, 0:S], Pr[0][:, 0:S], ACT.Square).then_inc(sem("kn_sq"), 1)
            act.wait_ge(job_done, J.val(2))
            fn(U3[0:ROPE, 0:S], pair(J + 1, p=ROPE), ACT.Copy, scale=col("q_norm_g_2", 1, ROPE)).then_inc(sem("qr_sb"), 1)
            fn(sqq[:, :], pair(J + 1, p=ROPE), ACT.Square).then_inc(*one(free(J + 1)))
            act.wait_ge(*free(J + 2))
            fn(sqk[:, S:NKEY], Pr[0][:, S:NKEY], ACT.Square).then_inc(sem("kn_sq"), 1)
            act.wait_ge(sem("qr_f"), h + 1)
            fn(QRh[:, :], U3[0:ROPE, 0:S], ACT.Copy).then_inc(sem("qr_hi"), 1)
            act.wait_ge(sem("kcols"), h + 1)
            fn(sd[:, 0:KT], PS[:, SC:SC + KT], ACT.Sqrt, scale=1.0 / QH, bias=eps_col).then_inc(sem("k_sd"), 1)
            act.wait_ge(job_done, J.val(4))
            fn(QNh[:, :], pair(J + 3), ACT.Copy, scale=col("q_norm_g_2", 0)).then_inc(sem("qn_hi"), 1)
            fn(Pr[1][:, 0:S], pair(J + 3), ACT.Square).then_inc(sem("qn_sq"), 1)
            act.wait_ge(sem("kn_f"), h + 1)
            fn(KNh[:, :], Pr[0][:, :], ACT.Copy).then_inc(sem("kn_hi"), 1)
            act.wait_ge(sem("kr_f"), h + 1)
            fn(KRh[:, :], U3[0:ROPE, :], ACT.Copy).then_inc(sem("kr_hi"), 1)
            for j, a, b in ((J + 4, 0, 8), (J + 5, 8, KT)):
                act.wait_ge(job_done, j.val(1))
                fn(Vh[:, a:b, :], pair(j, 0, (b - a) * P).rearrange("p (t n) -> p t n", n=P), ACT.Copy).then_inc(sem("v_hi"), 1)
            act.wait_ge(sem("head_var"), h + 1)
            fn(sd[:, 0:8], var[:, 0:8], ACT.Sqrt).then_inc(sem("head_sd"), 1)

            def exponentials(t):
                act.wait_ge(sem("nbias"), h * 8 + (t + 1))
                fn(Pr[t % 2][:, :], PS[:, 1536 * (t % 2):1536 * (t % 2) + NKEY], ACT.Exp,
                   scale=rqs[:, t:t + 1], bias=nbias[:, t % 2:t % 2 + 1],
                   accum_out=rsum[:, t % 2:t % 2 + 1]).then_inc(sem("p_exp"), 1)

            exponentials(0)
            exponentials(1)
            for g in range(4):
                if g >= 1:
                    act.wait_ge(sem("pv_done"), h * 4 + g)
                for t in (2 * g, 2 * g + 1):
                    for n, (k0, k1) in enumerate(((0, 4), (4, 8), (8, 10))):
                        o = 1536 * (t % 2)
                        act.wait_ge(sem("pt_pe"), h * 24 + (3 * t + n + 1))
                        fn(PTh[:, k0:k1, P * (t % 2):P * (t % 2 + 1)],
                           PS[:, o + k0 * P:o + k1 * P].rearrange("p (t n) -> p t n", n=P),
                           ACT.Copy).then_inc(sem("pt_hi_"), 1)
                if g < 3:
                    exponentials(2 * g + 2)
                    exponentials(2 * g + 3)
        act.wait_ge(sem("o_read"), 4 * HEADS)
        for h in range(HEADS):
            fn(XAh[:, h, :], ga[:, h, :], ACT.Copy).then_inc(sem("br_hi"), 1)
        for m in range(8):
            act.wait_ge(sem("yt_pe"), m + 1)
            if m >= 2:
                act.wait_ge(sem(f"out_done{m % 2}"), 16 * (m // 2))
            fn(onat[:, m % 2, :, :].rearrange("p t n -> p (t n)"), PS[:, ST:ST + S], ACT.Copy).then_inc(sem("on_ready"), 1)

    def vector_program(dve):
        tt, ts, stt = nc.vector.tensor_tensor, nc.vector.tensor_scalar, nc.vector.scalar_tensor_tensor

        marks = [0]

        def after_all(s, k):
            marks[0] += 1
            c = 58 + marks[0] % 6
            nc.vector.memset(small[:, c:c + 1], 0.0).then_inc(s, k)

        def rstd(n, width, cols, count, roots, dg=None, dcount=None, at_col=0, to=None):
            dve.wait_ge(sem("cols_pe"), cols)
            ts(var[:, 0:n], PS[:, SC + at_col:SC + at_col + n], 1.0 / width, EPS, ALU.mult, ALU.add).then_inc(sem("var"), 1)
            dve.wait_ge(sem("sd"), count)
            to = rcp[:, 0:n] if to is None else to
            nc.vector.reciprocal(to, sd[:, 0:n]).then_inc(sem("rcp"), 1)
            dve.wait_ge(sem("rcp"), roots)
            if dg is not None:
                diagonals(dg, n, to)

        def diagonals(dg, n, src):
            tt(dg, ident[:, :].unsqueeze(1).to_broadcast([P, n, P]), src.unsqueeze(2).to_broadcast([P, n, P]),
               ALU.mult).then_inc(sem("diag"), 1)

        nc.vector.memset(rows[:, :, :], 0.0).then_inc(sem("consts_set"), 1)
        nc.vector.memset(ones[:, :], 1.0).then_inc(sem("consts_set"), 1)
        dve.wait_ge(sem("g_in"), 16)
        for t in range(9):
            if t < 8:
                dve.wait_ge(sem("n1_sq"), t + 1)
                ts(var[:, t:t + 1], ssq[:, t:t + 1], 1.0 / D, EPS, ALU.mult, ALU.add).then_inc(sem("row_var"), 1)
                dve.wait_ge(sem("row_sd"), t + 1)
                nc.vector.reciprocal(rcp[:, t:t + 1], sd[:, t:t + 1]).then_inc(sem("row_rcp"), 1)
                dve.wait_ge(sem("row_rcp"), t + 1)
                if t >= 2:
                    dve.wait_ge(job_done, t - 1)
                stt(xs[:, t % 2, :], xn[:, t % 2, :], rcp[:, t:t + 1], gbc[:, :], ALU.mult, ALU.mult).then_inc(sem("xs_ready"), 1)
            if t >= 1:
                J = Lin(JOBS["x"] + t - 1)
                dve.wait_ge(sem("x_hi"), t)
                tt(XAl[:, :, (t - 1) * P:t * P], pair(J).rearrange("p (m n) -> p m n", n=P),
                   f32(XAh[:, :, (t - 1) * P:t * P]), ALU.subtract).then_inc(*one(free(J)))
        dve.wait_ge(sem("tab_pe"), 1)
        nc.vector.tensor_copy(tab[:, :], PS[:, ST:ST + 3 * P]).then_inc(sem("tab_ready"), 1)
        nc.vector.memset(gpad[:, :, 0:LPAD], 0.0).then_inc(sem("pads_zero"), 1)
        nc.vector.memset(T[1][:, 0:2], 0.0).then_inc(sem("pads_zero"), 1)
        nc.vector.memset(rbc[:, 0:8], 0.0).then_inc(sem("cv_ready"), 1)
        after_all(sem("modw_free"), 3)
        after_all(sem("mod_read"), 1)
        dve.wait_ge(sem("pads_zero"), 2)
        dve.wait_ge(sem("tab_ready"), 1)

        def tap(i, k, count):
            for a, b in ((0, H), (H, S)):
                if k == 0:
                    ts(tile(conv, i, a, b), tile(gpad, i, a, b), dcol("conv_a_w", i), dcol("conv_a_b", i),
                       ALU.mult, ALU.add).then_inc(sem("conv_tap"), 1)
                else:
                    dve.wait_ge(sem("conv_tap"), count * 2 + (a // H - 1))
                    stt(tile(conv, i, a, b), tile(gpad, i, k + a, k + b), dcol("conv_a_w", i + 4 * k),
                        tile(conv, i, a, b), ALU.mult, ALU.add).then_inc(sem("conv_tap"), 1)

        def read_mod(g):
            dve.wait_ge(sem("mod_pe"), g + 1)
            tt(mod_sb[:, ds(g * 4, 4), :], PS[:, SC + 64:SC + 72].rearrange("p (t n) -> p t n", n=2),
               tab[:, ds(g * 4 + COL["b_mod_2"], 4)].unsqueeze(2).to_broadcast([P, 4, 2]), ALU.add).then_inc(sem("mod_read"), 1)

        N1 = 14
        with dve.Fori(0, KC) as i:
            J = Lin(JOBS["glu"], 2, i)
            dve.wait_ge(*free(J))
            dve.wait_ge(job_done, J.val(2))
            tt(tile(gpad, i, LPAD, LPAD + S), pair(J + 1), T[0][:, 0:S], ALU.mult).then_inc(*one(free(J + 1)))
            dve.wait_ge(*free(J + 1))
            for k in range(N1):
                tap(i, k, i * N1 + k)
        N3 = 5
        N2 = TAPS_A - N1 - N3
        with dve.Fori(0, 2) as q:
            for u in range(2):
                i = q * 2 + u
                J = Lin(JOBS["short"] + 3 * u, 6, q)
                dve.wait_ge(job_done, J.val(2))
                dve.wait_ge(*free(J))
                tt(T[1][:, 2:2 + S], pair(J + 1), T[0][:, 0:S], ALU.mult).then_inc(*one(free(J + 1)))
                dve.wait_ge(*free(J + 1))
                ts(T[2][:, 0:S], T[1][:, 0:S], dcol("conv_b_w", i), None, ALU.mult).then_inc(sem("cv_ready"), 1)
                for k in range(1, TAPS_B):
                    if k == 1:
                        dve.wait_ge(sem("cv_ready"), q * 2 + (u + 2))
                    else:
                        dve.wait_ge(sem("short_tap"), q * 4 + (2 * u + k - 1))
                    stt(T[2][:, 0:S], T[1][:, k:k + S], dcol("conv_b_w", i + 4 * k), T[2][:, 0:S],
                        ALU.mult, ALU.add).then_inc(sem("short_tap"), 1)
                for k in range(N1, N1 + N2 // 2):
                    tap(i, k, i * N2 + (KC * N1 + k - N1))
                read_mod(q * 3 + u)
                dve.wait_ge(job_done, J.val(3))
                dve.wait_ge(sem("short_tap"), q * 4 + (2 * u + 2))
                tt(T[3][:, 0:S], pair(J + 2), T[2][:, 0:S], ALU.mult).then_inc(sem("s_ready"), 1)
                nc.vector.memset(T[1][:, 0:2], 0.0).then_inc(*one(free(J + 2)))
                for k in range(N1 + N2 // 2, N1 + N2):
                    tap(i, k, i * N2 + (KC * N1 + k - N1))
                if u == 1:
                    read_mod(q * 3 + 2)
                dve.wait_ge(sem("branch_hi"), q * 2 + (u + 1))
                tt(tile(XBl, q * 2 + (4 + u)), T[3][:, 0:S], f32(tile(XBh, q * 2 + (4 + u))),
                   ALU.subtract).then_inc(sem("branch_lo"), 1)

        def mix(name, a, b, add, taps=False):
            with dve.Fori(a, b) as m:
                J = Lin(JOBS[name], 2, m)
                dve.wait_ge(job_done, J.val(2))
                dve.wait_ge(*free(J))
                if not add:
                    tt(tile(R, m + (5 if a < 3 else -3)), pair(J + 1), T[0][:, 0:S], ALU.mult).then_inc(*one(free(J + 1)))
                    for v in range(2 if taps else 0):
                        i = m * 2 + v
                        for k in range(N1 + N2, TAPS_A):
                            tap(i, k, i * N3 + (KC * (N1 + N2) + k - N1 - N2))
                else:
                    tt(T[1][:, 0:S], pair(J + 1), T[0][:, 0:S], ALU.mult).then_inc(*one(free(J + 1)))
                    dve.wait_ge(*free(J + 1))
                    tt(tile(R, m), tile(R, m), T[1][:, 0:S], ALU.add).then_inc(sem("mix_done"), 1)
                    dve.wait_ge(sem("mix_done"), m + 1)

        v = [0]

        def ln_step(ins):
            v[0] += 1
            ins.then_inc(sem("ln_v"), 1)

        mix("mix_b", 0, 2, False, taps=True)
        dve.wait_ge(sem("conv_tap"), 2 * KC * TAPS_A)
        ln_step(tt(T[1][:, 0:S], conv[:, 0, :], conv[:, 1, :], ALU.add))
        for i in (2, 3):
            dve.wait_ge(sem("ln_v"), v[0])
            ln_step(tt(T[1][:, 0:S], T[1][:, 0:S], conv[:, i, :], ALU.add))
        mix("mix_b", 2, 3, False)
        dve.wait_ge(sem("ln_pe"), 1)
        for i in range(4):
            ln_step(stt(conv[:, i, :], PS[:, ST:ST + S], -1.0 / DC, conv[:, i, :], ALU.mult, ALU.add))
        dve.wait_ge(sem("ln_sq"), 2)
        ln_step(tt(T[1][:, 0:S], T[2][:, 0:S], T[3][:, 0:S], ALU.add))
        for i in (2, 3):
            dve.wait_ge(sem("ln_sq"), 1 + i)
            dve.wait_ge(sem("ln_v"), v[0])
            ln_step(tt(T[1][:, 0:S], T[1][:, 0:S], T[i][:, 0:S], ALU.add))
        mix("mix_b", 3, 5, False)
        rstd(8, DC, 1, 1, 1, T[2][:, 0:1024].rearrange("p (t n) -> p t n", n=P))
        mix("mix_b", 5, 7, False)
        dve.wait_ge(sem("rbc_ready"), 1)
        for i in range(5):
            if i < 4:
                if i >= 2:
                    dve.wait_ge(sem("a_silu"), i - 1)
                tt(T[1 + i % 2][:, 0:S], conv[:, i, :], rbc[:, :], ALU.mult).then_inc(sem("ln_n"), 1)
            if i >= 1:
                dve.wait_ge(sem("branch_hi"), 4 + i)
                dve.wait_ge(sem("ln_n"), i)
                tt(XBl[:, i - 1, :], T[3][:, 0:S], f32(XBh[:, i - 1, :]), ALU.subtract).then_inc(sem("branch_lo"), 1)
        mix("mix_b", 7, 8, False)
        mix("mix_a", 0, 8, True)
        for m in range(8):
            dve.wait_ge(sem("mx_hi"), m + 1)
            tt(XAl[:, m, :], R[:, m, :], f32(XAh[:, m, :]), ALU.subtract).then_inc(sem("mx_lo"), 1)
        nc.vector.memset(rbc[:, :], 0.0).then_inc(sem("ss_done0"), 1)
        dve.wait_ge(sem("ss_done0"), 1)
        after_all(sem("x2_ready"), 1)
        after_all(sem("ss_done"), 1)

        def residual_tail(m, hi, lo, sq, gname, mval, sbase):
            dve.wait_ge(sem(hi), mval)
            stt(tile(XBl, m), tile(R, m), dcol(gname, m), f32(tile(XBh, m)), ALU.mult, ALU.subtract).then_inc(sem(lo), 1)
            dve.wait_ge(sem(sq), mval)
            tt(rbc[:, :], rbc[:, :], T[3][:, 0:S], ALU.add).then_inc(sem("ss_done"), 1)

        with dve.Fori(0, KD // 2) as q:
            for u in range(2):
                m = q * 2 + u
                J = Lin(JOBS["wo"] + u, 2, q)
                dve.wait_ge(job_done, J.val(1))
                dve.wait_ge(sem("xt_sb"), q * 2 + (u + 1))
                tt(tile(R, m), pair(J), T[0][:, 0:S], ALU.add).then_inc(*one(free(J)))
                dve.wait_ge(*free(J))
                after_all(sem("x2_ready"), 1)
                residual_tail(m, "fx_hi", "fx_lo", "fx_sq", "g_ffn", q * 2 + (u + 1), 0)
                dve.wait_ge(sem("ss_done"), q * 2 + (u + 2))
        dve.wait_ge(sem("c_sq"), 2)
        ts(var[:, 0:2], csq[:, 0:2], 1.0 / D, EPS, ALU.mult, ALU.add).then_inc(sem("row_var"), 1)
        dve.wait_ge(sem("row_sd"), 9)
        nc.vector.reciprocal(rcp[:, 0:2], sd[:, 0:2]).then_inc(sem("row_rcp"), 1)
        dve.wait_ge(sem("row_rcp"), 9)
        for t in range(2):
            ts(cstage[:, t, :], cstage[:, t, :], rcp[:, t:t + 1], None, ALU.mult).then_inc(sem("cs_ready"), 1)
        for k in range(2):
            J = Lin(JOBS["p"] + k)
            dve.wait_ge(sem("pt_hi"), k + 1)
            tt(XAl[:, 4 + k, :], pair(J), f32(XAh[:, 4 + k, :]), ALU.subtract).then_inc(*one(free(J)))
        nc.vector.memset(T[0][:, 0:2], 0.0).then_inc(sem("pads_zero"), 1)
        rstd(8, D, 2, 2, 2, T[3][:, 0:1024].rearrange("p (t n) -> p t n", n=P))
        dve.wait_ge(sem("pads_zero"), 3)
        dve.wait_ge(sem("rbc_ready"), 2)

        def ffn_chunk(J, n, slot):
            for k in range(2):
                Jg = J + 2 * k
                dve.wait_ge(job_done, Jg.val(1))
                tt(T[0][:, 2:2 + S], pair(Jg), rbc[:, :], ALU.mult).then_inc(*one(free(Jg)))
                dve.wait_ge(*free(Jg))
                ts(T[1][:, 0:S], T[0][:, 0:S], dcol("conv_f_w", n + k), dcol("conv_f_b", n + k), ALU.mult, ALU.add).then_inc(sem("fc_tap"), 1)
                for w in range(1, TAPS_F):
                    dve.wait_ge(sem("fc_tap"), n * 3 + (3 * k + w))
                    stt(T[1][:, 0:S], T[0][:, w:w + S], dcol("conv_f_w", n + (k + NF * w)), T[1][:, 0:S],
                        ALU.mult, ALU.add).then_inc(sem("fc_tap"), 1)
                dve.wait_ge(job_done, Jg.val(2))
                tt(T[3][:, 0:S], pair(Jg + 1), rbc[:, :], ALU.mult).then_inc(*one(free(Jg + 1)))
                dve.wait_ge(*free(Jg + 1))
                dve.wait_ge(sem("gelu"), n + (k + 1))
                tt(T[3][:, 0:S], T[3][:, 0:S], T[2][:, 0:S], ALU.mult).then_inc(sem("f_ready"), 1)
                dve.wait_ge(sem("f_hi"), n + (k + 1))
                tt(XAl[:, 2 * slot + k, :], T[3][:, 0:S], f32(XAh[:, 2 * slot + k, :]), ALU.subtract).then_inc(sem("f_lo"), 1)

        def down(J):
            for m in range(8):
                dve.wait_ge(job_done, J.val(m + 1))
                tt(R[:, m, :], pair(J + m), R[:, m, :], ALU.add).then_inc(*one(free(J + m)))

        ffn_chunk(Lin(JOBS["ffn"]), 0, 0)
        with dve.Fori(0, (NCH - 1) // 2) as q:
            for u in range(2):
                J = Lin(JOBS["ffn_loop"] + 12 * u, 24, q)
                ffn_chunk(J, q * 4 + (2 * u + 2), 1 - u)
                down(J + 4)
        nc.vector.memset(rbc[:, :], 0.0).then_inc(sem("ss_done0"), 1)
        dve.wait_ge(sem("ss_done0"), 2)
        for m in range(KD + 1):
            if m < KD:
                J = Lin(JOBS["ffn_end"] + m)
                dve.wait_ge(job_done, J.val(1))
                tt(R[:, m, :], pair(J), R[:, m, :], ALU.add).then_inc(*one(free(J)))
            if m >= 1:
                dve.wait_ge(sem("fx_hi"), 8 + m)
                stt(XBl[:, m - 1, :], R[:, m - 1, :], col("g_ple", m - 1), f32(XBh[:, m - 1, :]), ALU.mult, ALU.subtract).then_inc(sem("fx_lo"), 1)
        dve.wait_ge(sem("fx_sq"), 16)
        tt(T[3][:, 0:S], T[1][:, 0:S], T[3][:, 0:S], ALU.add).then_inc(sem("ss_done0"), 1)
        dve.wait_ge(sem("ss_done0"), 3)
        dve.wait_ge(sem("ss_done"), KD + 7)
        tt(rbc[:, :], rbc[:, :], T[3][:, 0:S], ALU.add).then_inc(sem("ss_done"), 1)
        rstd(8, D, 3, 3, 3, T[3][:, 0:1024].rearrange("p (t n) -> p t n", n=P))
        nc.vector.memset(S1[:, :], 0.0).then_inc(sem("s12_done"), 1)
        nc.vector.memset(S2[:, :], 0.0).then_inc(sem("s12_done"), 1)
        dve.wait_ge(sem("rbc_ready"), 3)
        with dve.Fori(0, KD) as m:
            J = Lin(JOBS["ple"], 2, m)
            dve.wait_ge(job_done, J.val(1))
            tt(T[0][:, 0:S], pair(J), rbc[:, :], ALU.mult).then_inc(*one(free(J)))
            dve.wait_ge(job_done, J.val(2))
            dve.wait_ge(sem("pg_sig"), m + 1)
            tt(T[2][:, 0:S], pair(J + 1), T[1][:, 0:S], ALU.mult).then_inc(*one(free(J + 1)))
            dve.wait_ge(*free(J + 1))
            tt(tile(R, m), tile(R, m), T[2][:, 0:S], ALU.add).then_inc(sem("x4_ready"), 1)
            dve.wait_ge(sem("q12"), m * 2 + 2)
            dve.wait_ge(sem("s12_done"), m * 2 + 2)
            tt(S1[:, :], S1[:, :], Q1[:, :], ALU.add).then_inc(sem("s12_done"), 1)
            tt(S2[:, :], S2[:, :], Q2[:, :], ALU.add).then_inc(sem("s12_done"), 1)
        c = [0]

        def link(ins):
            c[0] += 1
            ins.then_inc(sem("chain"), 1)
            dve.wait_ge(sem("chain"), c[0])

        rf, rh = rql, rqs
        rstd(8, D, 5, 4, 4, to=rf)
        link(tt(tmp8, rf, rf, ALU.mult))
        link(tt(tmp8, PS[:, SC + 8:SC + 16], tmp8, ALU.mult))
        ts(var[:, 0:8], tmp8, 1.0 / D, EPS, ALU.mult, ALU.add).then_inc(sem("var"), 1)
        dve.wait_ge(sem("sd"), 5)
        link(nc.vector.reciprocal(tmp8, sd[:, 0:8]))
        link(tt(rh, rf, tmp8, ALU.mult))
        diagonals(Q1[:, :].rearrange("p (t n) -> p t n", n=P), 8, rh)
        diagonals(Q2[:, :].rearrange("p (t n) -> p t n", n=P), 8, rf)
        dve.wait_ge(sem("mod_read"), 7)
        gfc = tab[:, COL["g_final"]:COL["g_final"] + 8]
        ngc = tab[:, COL["norm_g_2"]:COL["norm_g_2"] + 8]
        link(ts(tmp8, mod_sb[:, 8:16, 0], 1.0, None, ALU.add))
        link(tt(tmp8, tmp8, ngc, ALU.mult))
        link(tt(Gx, tmp8, gfc, ALU.mult))
        link(ts(tmp8b, mod_sb[:, 8:16, 1], 1.0, None, ALU.add))
        link(tt(Gc, tmp8b, ngc, ALU.mult))
        dve.wait_ge(sem("rh_bc"), 1)
        for m in range(9):
            if m < 8:
                if m >= 2:
                    dve.wait_ge(sem("h_f"), m - 1)
                tt(T[m % 2][:, 0:S], R[:, m, :], rbc[:, :], ALU.mult).then_inc(sem("h_n"), 1)
            if m >= 1:
                dve.wait_ge(sem("h_hi"), m)
                tt(XBl[:, m - 1, :], T[2][:, 0:S], f32(XBh[:, m - 1, :]), ALU.subtract).then_inc(sem("h_lo"), 1)
        dve.wait_ge(sem("h_hi"), 9)
        tt(hcl[:, :, :], ctxT[:, :, :], f32(hch[:, :, :]), ALU.subtract).then_inc(sem("h_lo"), 1)
        dve.wait_ge(sem("rf_bc"), 1)
        for m in range(8):
            stt(R[:, m, :], R[:, m, :], col("g_final", m), T[3][:, 0:S], ALU.mult, ALU.mult).then_inc(sem("y_ready"), 1)
        dve.wait_ge(sem("kr_sb"), 2)
        after_all(*one(free(Lin(JOBS["mla_in"] + 2))))
        after_all(*one(free(Lin(JOBS["mla_in"] + 3))))
        dve.wait_ge(sem("rope_in"), 32)
        dve.wait_ge(sem("y_out"), 8 * 16)
        dve.wait_ge(sem("rot_pe"), 1)
        tt(U3[0:ROPE, 0:S], PS[0:ROPE, ST:ST + S], sinb[:, :], ALU.mult).then_inc(sem("krot_mul"), 1)
        tt(krot[:, 0:S], krT[:, 0:S], cosb[:, :], ALU.mult).then_inc(sem("krot_done"), 1)
        nc.vector.tensor_copy(krot[:, S:NKEY], krT[:, S:NKEY]).then_inc(sem("krot_done"), 1)
        dve.wait_ge(sem("krot_mul"), 1)
        dve.wait_ge(sem("krot_done"), 2)
        tt(krot[:, 0:S], krot[:, 0:S], U3[0:ROPE, 0:S], ALU.add).then_inc(sem("krot_done"), 1)
        for k in range(2):
            J = Lin(JOBS["mla_in"] + 4 + k)
            dve.wait_ge(sem("cq_hi"), k + 1)
            stt(CQl[:, k, :], pair(J), col("q_lora_g_2", k), f32(CQh[:, k, :]), ALU.mult, ALU.subtract).then_inc(sem("cq_lo"), 1)
            after_all(*one(free(J)))
        dve.wait_ge(sem("cq_sq"), 2)
        tt(cqs[:, 0, :], cqs[:, 0, :], cqs[:, 1, :], ALU.add).then_inc(sem("cq_ss"), 1)
        rstd(KT, 128, 6, 6, 5, dgck[:, :, :])
        dve.wait_ge(sem("bc_pe"), 6)
        stt(ckvT[:, :], ckvT[:, :], col("kv_lora_g_2", 0), PS[:, ST:ST + NKEY], ALU.mult, ALU.mult).then_inc(sem("ck_f"), 1)
        dve.wait_ge(sem("ck_hi"), 1)
        tt(CKl[:, :], ckvT[:, :], f32(CKh[:, :]), ALU.subtract).then_inc(sem("ck_lo"), 1)
        for x in (upad, wA, wB):
            nc.vector.memset(x[:, :], 0.0).then_inc(sem("pads2_zero"), 1)
        dve.wait_ge(sem("pads2_zero"), 3)
        n = [0]
        for gq in range(4):
            J = Lin(JOBS["pin"] + gq)
            dve.wait_ge(*free(J))
            src, ln = upad, TB // 4
            for s in range(gq + 1):
                dst = wA if s % 2 == 0 else wB
                sh = 1 << s
                ln -= sh
                if s:
                    dve.wait_ge(sem("win"), n[0])
                tt(dst[:, 0:ln], src[:, 0:ln], src[:, sh:sh + ln], ALU.add).then_inc(sem("win"), 1)
                n[0] += 1
                src = dst
            w = WINDOWS[gq]
            dve.wait_ge(sem("win"), n[0])
            dve.wait_ge(sem("inv_in"), 16 * (gq + 1))
            if gq >= 1:
                dve.wait_ge(sem("pool_lo"), gq)
                dve.wait_ge(sem("pool_hi"), gq)
            else:
                dve.wait_ge(sem("ck_lo"), 1)
            a = 8 - w // 2
            tt(pl[:, :], src[:, a:a + S], inv[:, :], ALU.mult).then_inc(sem("pl_mul"), 1)
            dve.wait_ge(sem("pl_mul"), gq + 1)
            tt(pl[:, :], pl[:, :], upad[:, 8:8 + S], ALU.subtract).then_inc(sem("pool_ready"), 1)
            dve.wait_ge(sem("pool_hi"), gq + 1)
            tt(XAl[:, 4 + gq, :], pl[:, :], f32(XAh[:, 4 + gq, :]), ALU.subtract).then_inc(sem("pool_lo"), 1)
            if gq == 0:
                rstd(8, 256, 7, 7, 6, at_col=16, to=rql)
        for gq in range(4):
            J = Lin(JOBS["pool"] + 2 * gq)
            dve.wait_ge(job_done, J.val(2))
            dve.wait_ge(*free(J))
            if gq == 0:
                dve.wait_ge(sem("pool_lo"), 4)
            else:
                dve.wait_ge(sem("pool_lo"), 4 + gq)
            stt(pl[:, :], pair(J + 1), col("pool_scale_2", gq), sgp[:, :], ALU.mult, ALU.mult).then_inc(sem("pool_ready"), 1)
            after_all(*one(free(J + 1)))
            dve.wait_ge(sem("pool_hi"), 4 + gq + 1)
            tt(XAl[:, 4 + gq, :], pl[:, :], f32(XAh[:, 4 + gq, :]), ALU.subtract).then_inc(sem("pool_lo"), 1)
        dve.wait_ge(sem("rope_in"), 64)
        nc.vector.memset(eps_col, EPS).then_inc(sem("k_ss"), 1)
        dve.wait_ge(sem("kr_sq"), 2)
        with dve.Fori(0, HEADS) as h:
            J = Lin(JOBS["heads"], 6, h)
            for j, a, b in ((J, 0, S), (J + 2, S, NKEY)):
                dve.wait_ge(job_done, j.val(1))
                nc.vector.tensor_copy(Pr[0][:, a:b], pair(j, 0, b - a)).then_inc(*one(free(j)))
            dve.wait_ge(sem("kn_sq"), h * 2 + 2)
            tt(sqk[0:ROPE, :], sqk[0:ROPE, :], sqkr[:, :], ALU.add).then_inc(sem("k_ss"), 1)
            dve.wait_ge(sem("qrot_pe"), h + 1)
            tt(dgq[:, :], PS[0:ROPE, ST:ST + S], sinq[:, :], ALU.mult).then_inc(sem("qr_a"), 1)
            tt(U3[0:ROPE, 0:S], U3[0:ROPE, 0:S], cosq[:, :], ALU.mult).then_inc(sem("qr_a"), 1)
            dve.wait_ge(sem("qr_a"), h * 2 + 2)
            tt(U3[0:ROPE, 0:S], U3[0:ROPE, 0:S], dgq[:, :], ALU.add).then_inc(sem("qr_f"), 1)
            dve.wait_ge(sem("qr_hi"), h + 1)
            dve.wait_ge(sem("qcols"), h * 2 + 1)
            tt(QRl[:, :], U3[0:ROPE, 0:S], f32(QRh[:, :]), ALU.subtract).then_inc(sem("qr_lo"), 1)

            dve.wait_ge(sem("k_sd"), h + 1)
            nc.vector.reciprocal(rcp[:, 0:KT], sd[:, 0:KT]).then_inc(sem("krcp"), 1)
            dve.wait_ge(sem("krcp"), h + 1)
            tt(dgh[:, :, :], ident[:, :].unsqueeze(1).to_broadcast([P, KT, P]),
               rcp[:, 0:KT].unsqueeze(2).to_broadcast([P, KT, P]), ALU.mult).then_inc(sem("kdiag"), 1)
            dve.wait_ge(sem("qn_hi"), h + 1)
            dve.wait_ge(sem("qn_sq"), h + 1)
            stt(QNl[:, :], pair(J + 3), col("q_norm_g_2", 0), f32(QNh[:, :]), ALU.mult, ALU.subtract).then_inc(*one(free(J + 3)))
            dve.wait_ge(sem("kbc"), h + 1)
            stt(Pr[0][:, :], Pr[0][:, :], col("k_norm_g_2", 0), PS[:, ST:ST + NKEY], ALU.mult, ALU.mult).then_inc(sem("kn_f"), 1)
            dve.wait_ge(sem("qr_lo"), h + 1)
            tt(U3[0:ROPE, :], krot[:, :], PS[0:ROPE, ST:ST + NKEY], ALU.mult).then_inc(sem("kr_f"), 1)
            dve.wait_ge(sem("kn_hi"), h + 1)
            tt(KNl[:, :], Pr[0][:, :], f32(KNh[:, :]), ALU.subtract).then_inc(sem("kn_lo"), 1)
            dve.wait_ge(sem("kr_hi"), h + 1)
            tt(KRl[:, :], U3[0:ROPE, :], f32(KRh[:, :]), ALU.subtract).then_inc(sem("kr_lo"), 1)
            for k, (j, a, b) in enumerate(((J + 4, 0, 8), (J + 5, 8, KT))):
                dve.wait_ge(sem("v_hi"), h * 2 + (k + 1))
                tt(Vl[:, a:b, :], pair(j, 0, (b - a) * P).rearrange("p (t n) -> p t n", n=P), f32(Vh[:, a:b, :]),
                   ALU.subtract).then_inc(sem("v_lo"), 1)
                after_all(*one(free(j)))
            dve.wait_ge(sem("qcols"), h * 2 + 2)
            nc.vector.tensor_copy(tmp8b, PS[:, SC + 48:SC + 56]).then_inc(sem("qf"), 1)
            dve.wait_ge(sem("qf"), h * 6 + 1)
            tt(tmp8, PS[:, SC + 16:SC + 24], tmp8b, ALU.add).then_inc(sem("qf"), 1)
            for n in (2, 3):
                dve.wait_ge(sem("qf"), h * 6 + n)
                tt(tmp8, tmp8, rql, ALU.mult).then_inc(sem("qf"), 1)
            dve.wait_ge(sem("qf"), h * 6 + 4)
            ts(var[:, 0:8], tmp8, 1.0 / QH, EPS, ALU.mult, ALU.add).then_inc(sem("head_var"), 1)
            dve.wait_ge(sem("head_sd"), h + 1)
            nc.vector.reciprocal(tmp8, sd[:, 0:8]).then_inc(sem("qf"), 1)
            dve.wait_ge(sem("qf"), h * 6 + 5)
            stt(rqs, tmp8, SCALE, rql, ALU.mult, ALU.mult).then_inc(sem("qf"), 1)
            dve.wait_ge(sem("qf"), h * 6 + 6)

            def maxima(t):
                a = t % 2
                dve.wait_ge(sem("s_done"), h * 8 + (t + 1))
                nc.vector.reduce_max(mx[:, a:a + 1], PS[:, 1536 * a:1536 * a + NKEY], AX.X).then_inc(sem("mx"), 1)
                dve.wait_ge(sem("mx"), h * 8 + (t + 1))
                stt(nbias[:, a:a + 1], mx[:, a:a + 1], -1.0, rqs[:, t:t + 1], ALU.mult, ALU.mult).then_inc(sem("nbias"), 1)

            def diagonal(t):
                a = t % 2
                dve.wait_ge(sem("p_exp"), h * 8 + (t + 1))
                nc.vector.reciprocal(rsum[:, a:a + 1], rsum[:, a:a + 1]).then_inc(sem("rs"), 1)
                dve.wait_ge(sem("rs"), h * 8 + (t + 1))
                ts(dgp[:, a, :], ident[:, :], rsum[:, a:a + 1], None, ALU.mult).then_inc(sem("p_diag"), 1)

            for t in range(2):
                maxima(t)
                diagonal(t)
            for g in range(4):
                for t in (2 * g, 2 * g + 1):
                    for n, (k0, k1) in enumerate(((0, 4), (4, 8), (8, 10))):
                        o = 1536 * (t % 2)
                        dve.wait_ge(sem("pt_hi_"), h * 24 + (3 * t + n + 1))
                        cols = slice(P * (t % 2), P * (t % 2 + 1))
                        tt(PTl[:, k0:k1, cols], PS[:, o + k0 * P:o + k1 * P].rearrange("p (t n) -> p t n", n=P),
                           f32(PTh[:, k0:k1, cols]), ALU.subtract).then_inc(sem("pt_lo"), 1)
                if g < 3:
                    for t in (2 * g + 2, 2 * g + 3):
                        maxima(t)
                        diagonal(t)
                dve.wait_ge(sem("pv_done"), h * 4 + (g + 1))
                part = tile(ga, h).rearrange("p (q t) -> p t q", t=8)[:, 2 * g:2 * g + 2, :]
                tt(part, PS[:, 3072:3072 + 2 * P].rearrange("p (t q) -> p t q", t=2), part, ALU.mult).then_inc(sem("o_read"), 1)
        for h in range(HEADS):
            dve.wait_ge(sem("br_hi"), h + 1)
            tt(XAl[:, h, :], ga[:, h, :], f32(XAh[:, h, :]), ALU.subtract).then_inc(sem("br_lo"), 1)
        for m in range(8):
            J = Lin(JOBS["out"] + m)
            dve.wait_ge(job_done, J.val(1))
            if m == 0:
                dve.wait_ge(sem("y_in"), 8 * 16)
            if m >= 2:
                dve.wait_ge(sem("yt_pe"), m - 1)
            stt(yout[:, m % 2, :], pair(J), mod_sb[:, 16 + m, 0:1], ybuf[:, m, :], ALU.mult, ALU.add).then_inc(sem("yo_ready"), 1)
            after_all(*one(free(J)))

    with nc.Block() as block:
        @block.sync
        def _(sp):
            sync_program(sp)

        @block.gpsimd
        def _(pool):
            pool_program(pool, SLABS["end"])

        @block.scalar
        def _(act):
            scalar_program(act)

        @block.tensor
        def _(pe):
            tensor_program(pe)

        @block.vector
        def _(dve):
            vector_program(dve)


_NAMES = ("x", "p", "g_mix", "w_in", "b_gate", "conv_a_w", "conv_a_b", "ln_a_g", "ln_a_b", "w_a_out", "conv_b_w",
          "w_b_out", "w_o", "g_ffn", "w_up", "conv_f_w", "conv_f_b", "w_down", "g_ple", "w_ple", "w_ple_gate",
          "g_final", "c_2", "ctx_2", "c_ctx_2", "w_mod_2", "b_mod_2", "norm_g_2", "w_in_2", "q_lora_g_2", "w_uq_2",
          "kv_lora_g_2", "w_ukv_2", "q_norm_g_2", "k_norm_g_2", "w_pool_2", "pool_scale_2", "w_out_2")


def shape_constants():
    import numpy as np
    pos = np.arange(S)
    inv = (np.float32(10000.0) ** (-np.arange(16, dtype=np.float32) / np.float32(16))).astype(np.float32)
    row = (pos // 64).astype(np.float32)[:, None] * inv
    column = (pos % 64).astype(np.float32)[:, None] * inv
    ang = np.concatenate([row, row, column, column], axis=-1)
    rot = np.zeros((ROPE, ROPE), np.float32)
    for half in (0, 32):
        for j in range(16):
            rot[half + 16 + j, half + j] = -1.0
            rot[half + j, half + 16 + j] = 1.0
    cnt = np.stack([np.clip(pos - w // 2 + w, 0, S) - np.clip(pos - w // 2, 0, S) for w in WINDOWS])
    return {
        "ident": np.eye(P, dtype=np.float32),
        "rotate": rot,
        "rope_cos": np.ascontiguousarray(np.cos(ang).T.astype(np.float32)),
        "rope_sin": np.ascontiguousarray(np.sin(ang).T.astype(np.float32)),
        "inv_cnt": (1.0 / cnt).astype(np.float32),
    }


def kernel(**inputs):
    import numpy as np
    import concourse.bacc as bacc
    from concourse.bass_utils import run_bass_kernel_spmd

    nc = bacc.Bacc("TRN2", target_bir_lowering=False, num_devices=1)
    arrays, A = {}, {}
    for name, a in [(n, inputs[n]) for n in _NAMES] + list(shape_constants().items()):
        a = np.ascontiguousarray(a)
        arrays[f"in_{name}"] = a
        A[name] = nc.dram_tensor(f"in_{name}", a.shape, mybir.dt.from_np(a.dtype), kind="ExternalInput").ap()
    out = nc.dram_tensor("out_x", (1, S, D), F32, kind="ExternalOutput").ap()
    ydram = nc.dram_tensor("y_scratch", (8, P, S), F32, kind="Internal").ap()
    build_program(nc, A, out, ydram)
    r = run_bass_kernel_spmd(nc, [arrays], core_ids=[0])
    return r.results[0]["out_x"]
```
